# Optimizing a Trainium2 kernel written in Bass

```python
import numpy as np
import jax
import jax.numpy as jnp
from jax import lax

D_MODEL = 1024
BATCH = 1
SEQ = 2048
DEPTH = 1

GRID_W = 64
CTX_LEN = 256

RET_HEAD_DIM = 128
RET_WIDTH = D_MODEL // 2
RET_HEADS = RET_WIDTH // RET_HEAD_DIM
RET_CHUNK = 128
RET_EPS = 1e-5
ROPE_BASE = 10000.0

RWKV_HEAD_DIM = 64
RWKV_WIDTH = D_MODEL // 2
RWKV_HEADS = RWKV_WIDTH // RWKV_HEAD_DIM
DECAY_LORA = 64
ICLR_LORA = 64
GATE_LORA = 128
RWKV_EPS = 64e-5

N_EXPERTS = 16
EXPERT_FF = 1024
CAPACITY_FACTOR = 2

N_MOD = 6
NORM_EPS = 1e-6

STATE_SIZES = (RET_WIDTH, RET_WIDTH, RWKV_WIDTH, RWKV_WIDTH, DECAY_LORA, ICLR_LORA)
QUERY_SIZES = (RET_WIDTH, RET_WIDTH, RWKV_WIDTH, GATE_LORA, 2 * D_MODEL)
STATE_COLS = sum(STATE_SIZES)
IN_COLS = STATE_COLS + sum(QUERY_SIZES)
SHIFT_STATE_COLS = 2 * RWKV_WIDTH + DECAY_LORA + ICLR_LORA
SHIFT_QUERY_COLS = RWKV_WIDTH + GATE_LORA
SHIFT_COLS = SHIFT_STATE_COLS + SHIFT_QUERY_COLS

kernel_name = 'hybrid_retention_rwkv7_ecmoe_dit_layer'

def _split(z, sizes):
    offs = np.cumsum((0,) + tuple(sizes))
    return [z[..., int(offs[i]):int(offs[i + 1])] for i in range(len(sizes))]

def _ident(a):
    return a

def _flip(a):
    return a[:, ::-1]

def _heads(a, dim):
    return a.reshape(a.shape[:-1] + (a.shape[-1] // dim, dim))

def _rmsnorm(x, g):
    xf = x.astype(jnp.float32)
    y = xf * lax.rsqrt(jnp.mean(xf * xf, axis=-1, keepdims=True) + NORM_EPS)
    return (y * g.astype(jnp.float32)).astype(x.dtype)

def _head_norm(x, eps):
    xf = x.astype(jnp.float32)
    mu = jnp.mean(xf, axis=-1, keepdims=True)
    var = jnp.mean(jnp.square(xf - mu), axis=-1, keepdims=True)
    y = (xf - mu) * lax.rsqrt(var + eps)
    return y.reshape(y.shape[:-2] + (-1,))

def _rope_2d(x):
    n = x.shape[1]
    t = jnp.arange(n)
    half = x.shape[-1] // 2
    nfreq = half // 2
    inv = ROPE_BASE ** (-jnp.arange(nfreq, dtype=jnp.float32) / nfreq)
    ang = jnp.concatenate([(t // GRID_W).astype(jnp.float32)[:, None] * inv,
                           (t % GRID_W).astype(jnp.float32)[:, None] * inv], axis=-1)
    cos = jnp.cos(ang)[None, :, None, :].astype(x.dtype)
    sin = jnp.sin(ang)[None, :, None, :].astype(x.dtype)
    x1, x2 = x[..., :half], x[..., half:]
    return jnp.concatenate([x1 * cos - x2 * sin, x1 * sin + x2 * cos], axis=-1)

def _centred_shift(p, mu):
    prev = jnp.pad(p[:, :-1], ((0, 0), (1, 0), (0, 0)))
    nxt = jnp.pad(p[:, 1:], ((0, 0), (0, 1), (0, 0)))
    return p + mu[0] * (prev - p) + mu[1] * (nxt - p)

def _retention_chunkwise(q, k, v, log_gamma, r0):
    b, t, h, _ = q.shape
    dv = v.shape[-1]
    n_chunks = t // RET_CHUNK
    lg = log_gamma.astype(jnp.float32)
    pos = jnp.arange(RET_CHUNK, dtype=jnp.float32)
    diff = pos[:, None] - pos[None, :]
    intra = jnp.where(diff >= 0, jnp.exp(lg[:, None, None] * jnp.maximum(diff, 0.0)), 0.0)
    cross = jnp.exp(lg[None, :] * (pos[:, None] + 1.0))
    tail = jnp.exp(lg[None, :] * (RET_CHUNK - 1.0 - pos[:, None]))
    chunk_decay = jnp.exp(lg * RET_CHUNK)

    def to_chunks(a):
        a = a.astype(jnp.float32).reshape(b, n_chunks, RET_CHUNK, h, a.shape[-1])
        return jnp.moveaxis(a, 1, 0)

    def step(r, xs):
        qc, kc, vc = xs
        s = jnp.einsum('bihd,bjhd->bhij', qc, kc) * intra
        o = (jnp.einsum('bhij,bjhe->bihe', s, vc)
             + jnp.einsum('bihd,bhde->bihe', qc, r) * cross[None, :, :, None])
        r = r * chunk_decay[None, :, None, None] + jnp.einsum('bjhd,bjhe->bhde', kc * tail[None, :, :, None], vc)
        return r, o

    r_final, o = lax.scan(step, r0.astype(jnp.float32), (to_chunks(q), to_chunks(k), to_chunks(v)))
    o = jnp.moveaxis(o, 0, 1).reshape(b, t, h, dv)
    return o.astype(v.dtype), r_final

def _retention_final_state(k, v, log_gamma):
    t = k.shape[1]
    w = jnp.exp(log_gamma[None, :] * (t - 1.0 - jnp.arange(t, dtype=jnp.float32)[:, None]))
    return jnp.einsum('bjhd,bjhe->bhde', k.astype(jnp.float32) * w[None, :, :, None], v.astype(jnp.float32))

def _rwkv7_scan(s0, w, k, v, kk, a, r=None):
    seq = [w, k, v, kk, a] + ([] if r is None else [r])
    xs = tuple(jnp.moveaxis(t.astype(jnp.float32), 1, 0) for t in seq)

    def step(s, xt):
        wt, kt, vt, kkt, at = xt[:5]
        sa = jnp.einsum('bhvk,bhk->bhv', s, -kkt)
        s = (s * wt[:, :, None, :] + sa[..., None] * (kkt * at)[:, :, None, :]
             + vt[..., None] * kt[:, :, None, :])
        if r is None:
            return s, None
        return s, jnp.einsum('bhvk,bhk->bhv', s, xt[5])

    s, ys = lax.scan(step, s0, xs)
    if r is None:
        return s, None
    return s, jnp.moveaxis(ys, 0, 1).astype(v.dtype)

def _side_state(h, lp, latent):
    z = h @ lp['w_in'][:, :STATE_COLS]
    ret_k, ret_v = _split(z[..., :2 * RET_WIDTH], (RET_WIDTH, RET_WIDTH))
    zr = _centred_shift(z[..., 2 * RET_WIDTH:], lp['rwkv_mu'][:, :SHIFT_STATE_COLS])
    k, v, wd, ad = _split(zr, (RWKV_WIDTH, RWKV_WIDTH, DECAY_LORA, ICLR_LORA))
    ret_k = _heads(ret_k, RET_HEAD_DIM) * (RET_HEAD_DIM ** -0.5)
    if latent:
        ret_k = _rope_2d(ret_k)
    kk = _heads(k * lp['rwkv_k_k'], RWKV_HEAD_DIM).astype(jnp.float32)
    kk = kk * lax.rsqrt(jnp.sum(kk * kk, axis=-1, keepdims=True) + 1e-12)
    u = lp['rwkv_w0'][:, None, None, :] + jnp.einsum('btr,drc->dbtc', jnp.tanh(wd), lp['rwkv_w2'])
    w = jnp.exp(-jnp.exp(-jax.nn.softplus(-u.astype(jnp.float32)) - 0.5))
    a = jax.nn.sigmoid(lp['rwkv_a0'][:, None, None, :] + jnp.einsum('btr,drc->dbtc', ad, lp['rwkv_a2']))
    k_dir = k[None] * (1.0 + (a - 1.0) * lp['rwkv_k_a'])
    return {'ret_k': ret_k, 'ret_v': _heads(ret_v, RET_HEAD_DIM), 'kk': kk,
            'w': _heads(w, RWKV_HEAD_DIM), 'a': _heads(a, RWKV_HEAD_DIM),
            'k': _heads(k_dir, RWKV_HEAD_DIM), 'v': _heads(v, RWKV_HEAD_DIM)}

def _side_query(h, lp, latent):
    z = h @ lp['w_in'][:, STATE_COLS:]
    ret_q, ret_g = _split(z[..., :2 * RET_WIDTH], (RET_WIDTH, RET_WIDTH))
    zr = _centred_shift(z[..., 2 * RET_WIDTH:2 * RET_WIDTH + SHIFT_QUERY_COLS], lp['rwkv_mu'][:, SHIFT_STATE_COLS:])
    r, gd = _split(zr, (RWKV_WIDTH, GATE_LORA))
    merge = z[..., 2 * RET_WIDTH + SHIFT_QUERY_COLS:]
    ret_q = _heads(ret_q, RET_HEAD_DIM)
    if latent:
        ret_q = _rope_2d(ret_q)
    return {'ret_q': ret_q, 'ret_g': ret_g, 'r': _heads(r, RWKV_HEAD_DIM),
            'rwkv_g': jax.nn.sigmoid(gd) @ lp['rwkv_g2'], 'merge': jax.nn.sigmoid(merge)}

def _branch_merge(ret_o, rwkv_o, st, qu, lp):
    dt = qu['ret_g'].dtype
    y_ret = (jax.nn.silu(qu['ret_g']) * (_head_norm(ret_o, RET_EPS) * lp['ret_gn_g']).astype(dt)) @ lp['w_br_ret']
    r_k = lp['rwkv_r_k'].reshape(RWKV_HEADS, RWKV_HEAD_DIM)
    bonus = jnp.sum(qu['r'][None] * st['k'] * r_k, axis=-1, keepdims=True).sum(0) * st['v']
    y_rw = (_head_norm(rwkv_o, RWKV_EPS) * lp['rwkv_ln_g'] + lp['rwkv_ln_b']).astype(dt)
    y_rw = ((y_rw + bonus.reshape(bonus.shape[:-2] + (-1,))) * qu['rwkv_g']) @ lp['w_br_rwkv']
    g_ret, g_rw = jnp.split(qu['merge'], 2, axis=-1)
    return (g_ret * y_ret + g_rw * y_rw) @ lp['w_out']

def _token_mixer(h_lat, h_ctx, lp, ctx_out):
    st_l = _side_state(h_lat, lp, True)
    qu_l = _side_query(h_lat, lp, True)
    st_c = _side_state(h_ctx, lp, False)
    qu_c = _side_query(h_ctx, lp, False) if ctx_out else None
    log_gamma = -jnp.exp(lp['ret_log_decay'].astype(jnp.float32))
    b = h_lat.shape[0]
    zero_ret = jnp.zeros((b, RET_HEADS, RET_HEAD_DIM, RET_HEAD_DIM), jnp.float32)
    zero_rw = jnp.zeros((b, RWKV_HEADS, RWKV_HEAD_DIM, RWKV_HEAD_DIM), jnp.float32)
    ret_l, rw_l, ret_c, rw_c = [], [], [], []
    for d, f in enumerate((_ident, _flip)):
        if ctx_out:
            o, r_state = _retention_chunkwise(f(qu_c['ret_q']), f(st_c['ret_k']), f(st_c['ret_v']), log_gamma[d], zero_ret)
            ret_c.append(f(o))
        else:
            r_state = _retention_final_state(f(st_c['ret_k']), f(st_c['ret_v']), log_gamma[d])
        o, _ = _retention_chunkwise(f(qu_l['ret_q']), f(st_l['ret_k']), f(st_l['ret_v']), log_gamma[d], r_state)
        ret_l.append(f(o))
        s_state, o = _rwkv7_scan(zero_rw, f(st_c['w'][d]), f(st_c['k'][d]), f(st_c['v']), f(st_c['kk']),
                                 f(st_c['a'][d]), f(qu_c['r']) if ctx_out else None)
        if ctx_out:
            rw_c.append(f(o))
        _, o = _rwkv7_scan(s_state, f(st_l['w'][d]), f(st_l['k'][d]), f(st_l['v']), f(st_l['kk']),
                           f(st_l['a'][d]), f(qu_l['r']))
        rw_l.append(f(o))
    y_lat = _branch_merge(ret_l[0] + ret_l[1], rw_l[0] + rw_l[1], st_l, qu_l, lp)
    y_ctx = _branch_merge(ret_c[0] + ret_c[1], rw_c[0] + rw_c[1], st_c, qu_c, lp) if ctx_out else None
    return y_lat, y_ctx

def _expert_choice_ffn(h, w_router, w_gate, w_up, w_down):
    b, n, d = h.shape
    cap = CAPACITY_FACTOR * n // N_EXPERTS
    aff = jax.nn.softmax((h @ w_router).astype(jnp.float32), axis=-1)
    gate, idx = lax.top_k(jnp.swapaxes(aff, 1, 2), cap)
    xg = jax.vmap(lambda hb, ib: hb[ib])(h, idx)
    hid = jax.nn.silu(jnp.einsum('becd,edf->becf', xg, w_gate)) * jnp.einsum('becd,edf->becf', xg, w_up)
    out = jnp.einsum('becf,efd->becd', hid, w_down) * gate[..., None].astype(h.dtype)
    return jax.vmap(lambda ob, ib: jnp.zeros((n, d), ob.dtype).at[ib.reshape(-1)].add(ob.reshape(-1, d)))(out, idx)

def setup_inputs(seed: int = 0) -> dict:
    key = jax.random.key(seed)
    ks = iter(jax.random.split(key, 32))
    f32 = jnp.float32

    def nrm(shape, scale):
        return scale * jax.random.normal(next(ks), shape, f32)

    L, D = DEPTH, D_MODEL
    ret_init = jnp.log(-jnp.log1p(-(2.0 ** (-5.0 - jnp.arange(RET_HEADS, dtype=f32)))))
    return {
        'x': nrm((BATCH, SEQ, D), 1.0),
        'c': nrm((BATCH, D), 1.0),
        'ctx': nrm((BATCH, CTX_LEN, D), 1.0),
        'c_ctx': nrm((D,), 1.0),
        'w_mod': nrm((L, D, N_MOD * D), 0.5 * D ** -0.5),
        'b_mod': nrm((L, N_MOD * D), 0.02),
        'norm_g': 1.0 + nrm((L, 4, D), 0.05),
        'w_in': nrm((L, D, IN_COLS), D ** -0.5),
        'ret_log_decay': ret_init[None, None, :] + nrm((L, 2, RET_HEADS), 0.1),
        'ret_gn_g': 1.0 + nrm((L, RET_WIDTH), 0.05),
        'rwkv_mu': jax.random.uniform(next(ks), (L, 2, SHIFT_COLS), f32, 0.0, 0.5),
        'rwkv_k_k': 0.85 + nrm((L, RWKV_WIDTH), 0.05),
        'rwkv_k_a': 1.0 + nrm((L, RWKV_WIDTH), 0.05),
        'rwkv_r_k': nrm((L, RWKV_WIDTH), 0.1),
        'rwkv_w0': jax.random.uniform(next(ks), (L, 2, RWKV_WIDTH), f32, -6.0, 0.0),
        'rwkv_w2': nrm((L, 2, DECAY_LORA, RWKV_WIDTH), 0.5 * DECAY_LORA ** -0.5),
        'rwkv_a0': nrm((L, 2, RWKV_WIDTH), 0.1),
        'rwkv_a2': nrm((L, 2, ICLR_LORA, RWKV_WIDTH), ICLR_LORA ** -0.5),
        'rwkv_g2': nrm((L, GATE_LORA, RWKV_WIDTH), GATE_LORA ** -0.5),
        'rwkv_ln_g': 1.0 + nrm((L, RWKV_WIDTH), 0.05),
        'rwkv_ln_b': nrm((L, RWKV_WIDTH), 0.02),
        'w_br_ret': nrm((L, RET_WIDTH, D), RET_WIDTH ** -0.5),
        'w_br_rwkv': nrm((L, RWKV_WIDTH, D), RWKV_WIDTH ** -0.5),
        'w_out': nrm((L, D, D), D ** -0.5),
        'w_router': nrm((L, D, N_EXPERTS), D ** -0.5),
        'w_gate': nrm((L, N_EXPERTS, D, EXPERT_FF), D ** -0.5),
        'w_up': nrm((L, N_EXPERTS, D, EXPERT_FF), D ** -0.5),
        'w_down': nrm((L, N_EXPERTS, EXPERT_FF, D), EXPERT_FF ** -0.5),
    }

def reference(x, c, ctx, c_ctx, w_mod, b_mod, norm_g, w_in, ret_log_decay, ret_gn_g, rwkv_mu,
              rwkv_k_k, rwkv_k_a, rwkv_r_k, rwkv_w0, rwkv_w2, rwkv_a0, rwkv_a2, rwkv_g2,
              rwkv_ln_g, rwkv_ln_b, w_br_ret, w_br_rwkv, w_out, w_router, w_gate, w_up, w_down):
    for l in range(DEPTH):
        last = l == DEPTH - 1
        lp = {'w_in': w_in[l], 'ret_log_decay': ret_log_decay[l], 'ret_gn_g': ret_gn_g[l],
              'rwkv_mu': rwkv_mu[l], 'rwkv_k_k': rwkv_k_k[l], 'rwkv_k_a': rwkv_k_a[l], 'rwkv_r_k': rwkv_r_k[l],
              'rwkv_w0': rwkv_w0[l], 'rwkv_w2': rwkv_w2[l], 'rwkv_a0': rwkv_a0[l], 'rwkv_a2': rwkv_a2[l],
              'rwkv_g2': rwkv_g2[l], 'rwkv_ln_g': rwkv_ln_g[l], 'rwkv_ln_b': rwkv_ln_b[l],
              'w_br_ret': w_br_ret[l], 'w_br_rwkv': w_br_rwkv[l], 'w_out': w_out[l]}
        ng = norm_g[l]
        sh1, sc1, g1, sh2, sc2, g2 = jnp.split((jax.nn.silu(c) @ w_mod[l] + b_mod[l])[:, None, :], N_MOD, axis=-1)
        csh1, csc1, cg1, csh2, csc2, cg2 = jnp.split(jax.nn.silu(c_ctx) @ w_mod[l] + b_mod[l], N_MOD, axis=-1)
        h_lat = _rmsnorm(x, ng[0]) * (1.0 + sc1) + sh1
        h_ctx = _rmsnorm(ctx, ng[0]) * (1.0 + csc1) + csh1
        y_lat, y_ctx = _token_mixer(h_lat, h_ctx, lp, not last)
        x = x + g1 * _rmsnorm(y_lat, ng[1])
        h2 = _rmsnorm(x, ng[2]) * (1.0 + sc2) + sh2
        x = x + g2 * _rmsnorm(_expert_choice_ffn(h2, w_router[l], w_gate[l], w_up[l], w_down[l]), ng[3])
        if not last:
            ctx = ctx + cg1 * _rmsnorm(y_ctx, ng[1])
            hc2 = _rmsnorm(ctx, ng[2]) * (1.0 + csc2) + csh2
            ctx = ctx + cg2 * _rmsnorm(_expert_choice_ffn(hc2, w_router[l], w_gate[l], w_up[l], w_down[l]), ng[3])
    return x


_drawn_inputs = setup_inputs


def setup_inputs(seed=0):
    import zlib

    import numpy as np

    out = dict(_drawn_inputs(seed))
    spreads = {}
    factors = {'rwkv_ln_b': 7.867, 'rwkv_a0': 3.592, 'rwkv_w2': 2.667}
    for name, (base, spread) in spreads.items():
        noise = np.random.default_rng([zlib.crc32(name.encode()), seed]).standard_normal(out[name].shape)
        drawn = base * np.exp(spread * noise) if base else spread * noise
        out[name] = jnp.asarray(drawn.astype(out[name].dtype))
    for name, factor in factors.items():
        out[name] = (out[name] * factor).astype(out[name].dtype)
    return out
```

```python
from contextlib import ExitStack

import numpy as np
import concourse.bass as bass
from concourse import mybir

F32 = mybir.dt.float32
F32R = mybir.dt.float32r
BF16 = mybir.dt.bfloat16
I32 = mybir.dt.int32
U32 = mybir.dt.uint32
ALU = mybir.AluOpType
ACT = mybir.ActivationFunctionType
AX = mybir.AxisListType

P = 128
D = 1024
KT = D // P
CTX, LAT = 256, 2048
TOK = CTX + LAT
NT = TOK // P
CT = CTX // P
RH, RD = 4, 128
WH, WD = 8, 64
HALF = 512
NE, CAP, FF = 16, 256, 1024
MOD = 6 * D
EPS = 1e-6
RET_EPS, RWKV_EPS = 1e-5, 64e-5
DEC = float(np.exp(-0.5))
ds = bass.ds

Z_RK, Z_RV, Z_K, Z_V, Z_WA, Z_GD, Z_RQ, Z_R, Z_RG, Z_MG = 0, 4, 8, 12, 16, 17, 18, 22, 26, 30
NZ = 46


START = 1


class Room:

    def __init__(self, nc, tag, start=START):
        self.nc, self.tag, self.start, self.stack, self.sems = nc, tag, start, ExitStack(), []

    def __enter__(self):
        self.stack.__enter__()
        return self

    def __exit__(self, *a):
        done = self.stack.__exit__(*a)
        if self.sems:
            self.nc.clear_and_free_semaphores([sem for sem, _ in self.sems])
            self.nc.all_engine_barrier()
        return done

    def sb(self, name, shape, dt=F32):
        return self.stack.enter_context(self.nc.sbuf_tensor(f"{self.tag}__{name}", list(shape), dt))

    def ps(self, name, shape, dt=F32):
        return self.stack.enter_context(self.nc.psum_tensor(f"{self.tag}__{name}", list(shape), dt))

    def sem(self, name, start=None):
        self.sems.append((self.nc.alloc_semaphore(f"{self.tag}__{name}"), self.start if start is None else start))
        return self.sems[-1][0]

    def block(self):
        for sem, start in self.sems:
            if start:
                self.nc.gpsimd.sem_inc(sem, start)
        if self.start:
            self.nc.all_engine_barrier()
        return self.stack.enter_context(self.nc.Block())


class Steps:

    def __init__(self, eng, sem, base=0):
        self.eng, self.sem, self.base, self.n = eng, sem, base, 0

    def done(self, ins):
        self.n += 1
        return ins.then_inc(self.sem, 1)

    def wait(self):
        self.eng.wait_ge(self.sem, self.base + self.n + START)


def product(pe, out, stat, mov, first, last):
    (sh, sl), (mh, ml) = stat, mov
    pe.matmul(out, sh, mh, start=first, stop=False)
    pe.matmul(out, sl, mh, start=False, stop=False)
    return pe.matmul(out, sh, ml, start=False, stop=last)


def modulation(nc, T):
    NB, W = MOD // 512, 512
    with Room(nc, "mod") as room:
        cond = room.sb("cond", [P, KT, 2])
        act_c = room.sb("act_c", [P, KT, 2])
        bias = room.sb("bias", [2, MOD])
        rows = room.sb("rows", [2, MOD])
        w = [room.sb(f"w{u}", [P, KT, W]) for u in range(2)]
        acc = [room.ps(f"acc{u}", [2, W]) for u in range(2)]
        c_in, b_in, silu_done = room.sem("c_in"), room.sem("b_in"), room.sem("silu_done")
        w_in = [room.sem(f"w_in{u}") for u in range(2)]
        used, row_done, out_done = room.sem("used"), room.sem("row_done"), room.sem("out_done")
        wm = T["w_mod"]
        block = room.block()

        @block.sync
        def _(sp):
            with nc.allow_non_contiguous_dma("conditioning vectors, model width over partitions"):
                sp.dma_start(cond[:, :, 0], T["c"].rearrange("a (t p) -> p (a t)", p=P)).then_inc(c_in, 16)
                sp.dma_start(cond[:, :, 1], T["c_ctx"].rearrange("(t p) -> p t", p=P)).then_inc(c_in, 16)
            for r in range(2):
                sp.dma_start(bias[r:r + 1, :], T["b_mod"]).then_inc(b_in, 16)
            for u in range(2):
                sp.dma_start(w[u][:, :, :], wm[u]).then_inc(w_in[u], 16)
            with sp.Fori(0, NB // 2 - 1) as i:
                for u in range(2):
                    sp.wait_ge(used, i * 2 + (u + 1) + START)
                    sp.dma_start(w[u][:, :, :], wm[ds(i * 2 + (u + 2), 1)]).then_inc(w_in[u], 16)
            sp.wait_ge(row_done, NB + START)
            sp.dma_start(T["mod_rows"], rows[:, :]).then_inc(out_done, 16)
            sp.wait_ge(out_done, 16 + START)

        @block.scalar
        def _(act):
            act.wait_ge(c_in, 32 + START)
            act.activation(act_c[:, :, :], cond[:, :, :], ACT.Silu).then_inc(silu_done, 1)

        @block.tensor
        def _(pe):
            pe.wait_ge(silu_done, 1 + START)
            with pe.Fori(0, NB // 2) as i:
                for u in range(2):
                    pe.wait_ge(w_in[u], i * 16 + 16 + START)
                    pe.wait_ge(row_done, i * 2 + START)
                    for k in range(KT):
                        mm = pe.matmul(acc[u][:, :], act_c[:, k, :], w[u][:, k, :], start=(k == 0), stop=(k == KT - 1))
                    mm.then_inc(used, 1)

        @block.vector
        def _(ve):
            ve.wait_ge(b_in, 32 + START)
            with ve.Fori(0, NB // 2) as i:
                for u in range(2):
                    at = ds(i * (2 * W) + u * W, W)
                    ve.wait_ge(used, i * 2 + (u + 1) + START)
                    ve.tensor_tensor(rows[:, at], acc[u][:, :], bias[:, at], ALU.add).then_inc(row_done, 1)


def projection(nc, T):
    with Room(nc, "prj") as room:
        ident = room.sb("ident", [P, P])
        rowmod = room.sb("rowmod", [P, 3, KT, 2])
        gain = room.sb("gain", [P, KT])
        scale = room.sb("scale", [P, KT, 2])
        hT = [room.sb("hT_hi", [P, KT, TOK], F32R), room.sb("hT_lo", [P, KT, TOK], F32R)]
        with Room(nc, "nrm") as r1:
            xin = [r1.sb(f"xin{u}", [P, D]) for u in range(2)]
            xn = [r1.sb(f"xn{u}", [P, D]) for u in range(2)]
            sq = r1.sb("sq", [P, D])
            hv = [r1.sb(f"hv{u}", [P, KT, P]) for u in range(2)]
            ss = [r1.sb(f"ss{u}", [P, 1]) for u in range(2)]
            rt = [r1.sb(f"rt{u}", [P, 1]) for u in range(2)]
            rs = [r1.sb(f"rs{u}", [P, 1]) for u in range(2)]
            epsc = r1.sb("epsc", [P, 1])
            tp = [r1.ps(f"tp{u}", [P, KT, P]) for u in range(2)]
            const_in, ready = r1.sem("const_in"), r1.sem("ready")
            x_in = [r1.sem(f"x_in{u}") for u in range(2)]
            root, norm, turned, moved = r1.sem("root"), r1.sem("norm"), r1.sem("turned"), r1.sem("moved")
            hi_done, lo_done, sums, steps, recips = r1.sem("hi_done"), r1.sem("lo_done"), r1.sem("sums"), r1.sem("steps"), r1.sem("recips")
            block = r1.block()
            src = T["tokens"].rearrange("(n p) d -> n p d", p=P)

            @block.sync
            def _(sp):
                sp.dma_start(ident[:, :], T["ident"]).then_inc(const_in, 16)
                with nc.allow_non_contiguous_dma("modulation, model width over partitions"):
                    for r in range(2):
                        for which in range(2):
                            sp.dma_start(rowmod[:, which, :, r],
                                         T["mod_rows"][r:r + 1, which * D:(which + 1) * D]
                                         .rearrange("a (t p) -> p (a t)", p=P)).then_inc(const_in, 16)
                    sp.dma_start(gain[:, :], T["norm_g"][0, 0:1, :].rearrange("a (t p) -> p (a t)", p=P)).then_inc(const_in, 16)
                for u in range(2):
                    sp.dma_start(xin[u][:, :], src[u]).then_inc(x_in[u], 16)
                with sp.Fori(0, NT // 2 - 1) as i:
                    for u in range(2):
                        sp.wait_ge(norm, i * 2 + (u + 1) + START)
                        sp.dma_start(xin[u][:, :], src[ds(i * 2 + (u + 2), 1)]).then_inc(x_in[u], 16)

            def tiles(eng, body):
                body(0, 1)
                with eng.Fori(1, NT // 2) as i:
                    body(i, 0)

            @block.scalar
            def _(act):
                act.wait_ge(ready, 1 + START)

                def body(i, which):
                    for u in range(2):
                        act.wait_ge(x_in[u], i * 16 + 16 + START)
                        act.activation(sq[:, :], xin[u][:, :], ACT.Square, accum_out=ss[u][:, :]).then_inc(sums, 1)
                        act.wait_ge(sums, i * 2 + (u + 1) + START)
                        act.activation(rt[u][:, :], ss[u][:, :], ACT.Sqrt, scale=1.0 / D, bias=epsc[:, :]).then_inc(root, 1)
                    for u in range(2):
                        act.wait_ge(moved, i * 2 + (u + 1) + START)
                        act.activation(hT[0][:, :, ds(i * (2 * P) + u * P, P)], hv[u][:, :, :], ACT.Copy).then_inc(hi_done, 1)
                tiles(act, body)

            @block.tensor
            def _(pe):
                pe.wait_ge(const_in, 16 * 6 + START)

                def body(i, which):
                    for u in range(2):
                        pe.wait_ge(norm, i * 2 + (u + 1) + START)
                        pe.wait_ge(moved, i * 2 + START)
                        for k in range(KT):
                            t = pe.transpose(tp[u][:, k, :], xn[u][:, k * P:(k + 1) * P], ident[:, :])
                        t.then_inc(turned, 1)
                tiles(pe, body)

            @block.vector
            def _(ve):
                st = Steps(ve, steps)
                ve.memset(epsc[:, :], EPS)
                ve.wait_ge(const_in, 16 * 6 + START)
                st.done(ve.tensor_scalar(rowmod[:, 2, :, :], rowmod[:, 1, :, :], 1.0, None, ALU.add))
                st.wait()
                for r in range(2):
                    last = st.done(ve.tensor_tensor(scale[:, :, r], rowmod[:, 2, :, r], gain[:, :], ALU.mult))
                st.wait()
                ve.sem_inc(ready, 1)

                def body(i, which):
                    for u in range(2):
                        ve.wait_ge(root, i * 2 + (u + 1) + START)
                        ve.reciprocal(rs[u][:, :], rt[u][:, :]).then_inc(recips, 1)
                    for u in range(2):
                        ve.wait_ge(recips, i * 2 + (u + 1) + START)
                        ve.wait_ge(turned, i * 2 + START)
                        ve.tensor_scalar(xn[u][:, :], xin[u][:, :], rs[u][:, 0:1], None, ALU.mult).then_inc(norm, 1)
                    for u in range(2):
                        ve.wait_ge(turned, i * 2 + (u + 1) + START)
                        ve.wait_ge(lo_done, i * 2 + START)
                        ve.wait_ge(hi_done, i * 2 + START)
                        for k in range(KT):
                            mv = ve.tensor_scalar(hv[u][:, k, :], tp[u][:, k, :], scale[:, k, which:which + 1],
                                                  rowmod[:, 0, k, which:which + 1], ALU.mult, ALU.add)
                        mv.then_inc(moved, 1)
                    for u in range(2):
                        at = ds(i * (2 * P) + u * P, P)
                        ve.wait_ge(hi_done, i * 2 + (u + 1) + START)
                        ve.tensor_tensor(hT[1][:, :, at], hv[u][:, :, :], hT[0][:, :, at], ALU.subtract).then_inc(lo_done, 1)
                tiles(ve, body)

        with Room(nc, "zp") as r2:
            w = [r2.sb(f"w{u}", [P, KT, P]) for u in range(2)]
            wh = [r2.sb(f"wh{u}", [P, KT, P], F32R) for u in range(2)]
            wl = [r2.sb(f"wl{u}", [P, KT, P], F32R) for u in range(2)]
            zo = [r2.sb(f"zo{u}", [P, TOK]) for u in range(2)]
            acc = [r2.ps(f"acc{b}", [P, 512]) for b in range(5)]
            w_in, stored = [[r2.sem(f"{n}{u}") for u in range(2)] for n in ("w_in", "stored")]
            spent, split_hi, split_lo, made, kept = r2.sem("spent"), r2.sem("split_hi"), r2.sem("split_lo"), r2.sem("made"), r2.sem("kept")
            block = r2.block()
            BLOCKS = [(0, CTX)] + [(CTX + 512 * b, 512) for b in range(4)]
            RUNS = [(0, 18, 0, ACT.Copy), (18, 8, 1, ACT.Copy), (26, 4, 1, ACT.Silu), (30, 16, 1, ACT.Sigmoid)]
            wz = T["w_z"]
            zT = T["zT"].rearrange("(n p) t -> n p t", p=P)

            def runs(eng, body):
                before = 0
                for t0, n, b0, fn in RUNS:
                    nb = 5 - b0
                    first = t0 // 2
                    if t0 == 0:
                        body(0, 0, b0, fn)
                        first = 1
                    with eng.Fori(first, (t0 + n) // 2) as i:
                        body(i, i * (2 * nb) + (before - t0 * nb), b0, fn)
                    before += n * nb

            @block.sync
            def _(sp):
                for u in range(2):
                    sp.dma_start(w[u][:, :, :], wz[u]).then_inc(w_in[u], 16)

                def body(i, g, b0, fn):
                    lo = BLOCKS[b0][0]
                    for u in range(2):
                        sp.wait_ge(split_lo, i * 2 + (u + 1) + START)
                        sp.sem_inc(spent, 1)
                        sp.dma_start(w[u][:, :, :], wz[ds(i * 2 + (u + 2), 1)]).then_inc(w_in[u], 16)
                        sp.wait_ge(kept, g + (u + 1) * (5 - b0) + START)
                        sp.sem_inc(spent, 1)
                        sp.dma_start(zT[ds(i * 2 + u, 1), :, lo:TOK], zo[u][:, lo:TOK]).then_inc(stored[u], 16)
                runs(sp, body)
                for u in range(2):
                    sp.wait_ge(stored[u], 8 * NZ + START)

            @block.scalar
            def _(act):
                def split_high(u, i):
                    act.wait_ge(w_in[u], i * 16 + 16 + START)
                    act.activation(wh[u][:, :, :], w[u][:, :, :], ACT.Copy).then_inc(split_hi, 1)

                def body(i, g, b0, fn):
                    for u in range(2):
                        if not isinstance(i, int):
                            act.wait_ge(stored[u], i * 16 + START)
                        for b in range(b0, 5):
                            lo, n = BLOCKS[b]
                            act.wait_ge(made, g + (u * (5 - b0) + b - b0 + 1) + START)
                            act.activation(zo[u][:, lo:lo + n], acc[b][:, 0:n], fn).then_inc(kept, 1)
                        split_high(u, i + 1)
                for u in range(2):
                    split_high(u, 0)
                runs(act, body)

            @block.vector
            def _(ve):
                with ve.Fori(0, NZ // 2 + 1) as i:
                    for u in range(2):
                        ve.wait_ge(split_hi, i * 2 + (u + 1) + START)
                        ve.tensor_tensor(wl[u][:, :, :], w[u][:, :, :], wh[u][:, :, :], ALU.subtract).then_inc(split_lo, 1)

            @block.tensor
            def _(pe):
                def body(i, g, b0, fn):
                    for u in range(2):
                        pe.wait_ge(split_lo, i * 2 + (u + 1) + START)
                        for b in range(b0, 5):
                            lo, n = BLOCKS[b]
                            j = u * (5 - b0) + b - b0
                            if u or not isinstance(i, int):
                                pe.wait_ge(kept, g + (j - (4 - b0)) + START)
                            for k in range(KT):
                                mm = product(pe, acc[b][:, 0:n], (wh[u][:, k, :], wl[u][:, k, :]),
                                             (hT[0][:, k, lo:lo + n], hT[1][:, k, lo:lo + n]), k == 0, k == KT - 1)
                            mm.then_inc(made, 1)
                runs(pe, body)


def rwkv_channels(nc, T):
    W = TOK + 1
    SEGS = [(0, CTX, 0), (CTX + 1, W, CTX)]
    with Room(nc, "rch", start=0) as room:
        sb, sem = room.sb, room.sem
        ones = sb("ones", [P, P])
        g2 = sb("g2", [P, HALF])
        mu = sb("mu", [P, 14, 2])
        keep = sb("keep", [P, 14])
        par = sb("par", [P, 3, 4])
        tiny = sb("tiny", [P, 1])
        X = [sb(f"X{u}", [P, W + 2]) for u in range(3)]
        Y = [sb(f"Y{u}", [P, W]) for u in range(2)]
        norm = sb("norm", [P, W])
        ks = sb("ks", [P, W])
        kkn = sb("kkn", [P, W])
        kka = sb("kka", [P, W])
        rrk = sb("rrk", [P, W])
        gate = [sb(f"gate{u}", [P, TOK]) for u in range(2)]
        acc = room.ps("acc", [P, 5, 512])
        const_in, zeroed, keep_ok = sem("const_in"), sem("zeroed"), sem("keep_ok")
        x_in = [sem(f"x_in{u}") for u in range(3)]
        scaled, half, shifted = sem("scaled"), sem("half"), sem("shifted")
        squared, summed, rooted, ks_ok, kka_ok, recip, kkn_ok = [sem(n) for n in (
            "squared", "summed", "rooted", "ks_ok", "kka_ok", "recip", "kkn_ok")]
        rrk_ok, tanh_ok, sig_ok, g_made, g_ok = [sem(n) for n in ("rrk_ok", "tanh_ok", "sig_ok", "g_made", "g_ok")]
        y_out = [sem(f"y_out{u}") for u in range(2)]
        kkn_out, kka_out, rrk_out = sem("kkn_out"), sem("kka_out"), sem("rrk_out")
        g_out = [sem(f"g_out{u}") for u in range(2)]
        BL = [(512 * b, min(512, W - 512 * b)) for b in range(5)]
        zT = T["zT"].rearrange("(n p) t -> n p t", p=P)
        tiled = {n: T[n].rearrange("(n p) t -> n p t", p=P) for n in ("kS", "kkn", "kka", "vS", "rS", "rrk", "gT")}
        JOBS = [("wa", 0, Z_WA, 8), ("gd", 0, Z_GD, 13)]
        for p in range(4):
            JOBS += [("k", p, Z_K + p, p), ("r", p, Z_R + p, 9 + p), ("v", p, Z_V + p, 4 + p)]
        xbuf = [2 if kind == "r" else None for kind, *_ in JOBS]
        for n, j in enumerate(j for j, x in enumerate(xbuf) if x is None):
            xbuf[j] = n % 2

        def earlier(j, same):
            return max((i for i in range(j) if same[i] == same[j]), default=None)

        def loaded(j):
            return sum(16 if JOBS[i][0] == "r" else 32 for i in range(j + 1) if xbuf[i] == xbuf[j])

        def y_stored(j):
            return sum({"gd": 0}.get(JOBS[i][0], 32) for i in range(j % 2, j + 1, 2))
        block = room.block()

        @block.sync
        def _(sp):
            sp.dma_start(ones[:, :], T["head_ones"]).then_inc(const_in, 16)
            sp.dma_start(g2[:, :], T["rwkv_g2"][0]).then_inc(const_in, 16)
            with nc.allow_non_contiguous_dma("channel parameters over partitions"):
                for r in range(2):
                    sp.dma_start(mu[:, :, r], T["rwkv_mu"][0, r:r + 1, :].rearrange("a (t p) -> p (a t)", p=P)).then_inc(const_in, 16)
                for j, n in enumerate(("rwkv_k_k", "rwkv_k_a", "rwkv_r_k")):
                    sp.dma_start(par[:, j, :], T[n].rearrange("a (t p) -> p (a t)", p=P)).then_inc(const_in, 16)
            sp.wait_ge(zeroed, 3)
            for j, (kind, p, row, _) in enumerate(JOBS):
                before = earlier(j, xbuf)
                if before is not None:
                    sp.wait_ge(shifted, before + 1)
                x = X[xbuf[j]]
                for lo, hi, d in SEGS[kind == "r":]:
                    sp.dma_start(x[:, 1 + lo:1 + hi], zT[row, :, d:d + hi - lo]).then_inc(x_in[xbuf[j]], 16)

        @block.vector
        def _(ve):
            for x in X:
                ve.memset(x[:, :], 0.0).then_inc(zeroed, 1)
            ve.memset(tiny[:, :], 1e-12).then_inc(zeroed, 1)
            ve.wait_ge(const_in, 16 * 7)
            ve.tensor_tensor(keep[:, :], mu[:, :, 0], mu[:, :, 1], ALU.add).then_inc(zeroed, 1)
            ve.wait_ge(zeroed, 5)
            ve.tensor_scalar(keep[:, :], keep[:, :], -1.0, 1.0, ALU.mult, ALU.add).then_inc(keep_ok, 1)
            nk = 0
            for j, (kind, p, row, m) in enumerate(JOBS):
                x, y = X[xbuf[j]], Y[j % 2]
                ve.wait_ge(scaled, j + 1)
                ve.scalar_tensor_tensor(y[:, :], x[:, 0:W], mu[:, m, 0:1], y[:, :], ALU.mult, ALU.add).then_inc(half, 1)
                ve.wait_ge(half, j + 1)
                ve.scalar_tensor_tensor(y[:, :], x[:, 2:2 + W], mu[:, m, 1:2], y[:, :], ALU.mult, ALU.add).then_inc(shifted, 1)
                if j and JOBS[j - 1][0] == "k":
                    nk += 1
                    ve.wait_ge(rooted, nk)
                    ve.reciprocal(norm[:, :], norm[:, :]).then_inc(recip, 1)
                    ve.wait_ge(recip, nk)
                    ve.wait_ge(ks_ok, nk)
                    if nk > 1:
                        ve.wait_ge(kkn_out, 32 * (nk - 1))
                    ve.scalar_tensor_tensor(kkn[:, :], ks[:, :], -1.0, norm[:, :], ALU.mult, ALU.mult).then_inc(kkn_ok, 1)

        @block.scalar
        def _(act):
            act.wait_ge(const_in, 16 * 7)
            act.wait_ge(keep_ok, 1)
            nk = nr = 0
            for j, (kind, p, row, m) in enumerate(JOBS):
                x, y = X[xbuf[j]], Y[j % 2]
                act.wait_ge(x_in[xbuf[j]], loaded(j))
                if j >= 2:
                    act.wait_ge(y_out[j % 2], y_stored(j - 2))
                    if JOBS[j - 2][0] == "gd":
                        act.wait_ge(g_made, 16)
                act.activation(y[:, :], x[:, 1:1 + W], ACT.Copy, scale=keep[:, m:m + 1]).then_inc(scaled, 1)
                if j and JOBS[j - 1][0] == "k":
                    act.wait_ge(summed, nk)
                    act.activation(norm[:, :], acc[:, :, :].rearrange("p a b -> p (a b)")[:, 0:W], ACT.Sqrt, bias=tiny[:, :]).then_inc(rooted, 1)
                act.wait_ge(shifted, j + 1)
                if kind == "k":
                    nk += 1
                    if nk > 1:
                        act.wait_ge(kkn_ok, nk - 1)
                        act.wait_ge(kka_out, 32 * (nk - 1))
                    act.activation(norm[:, :], y[:, :], ACT.Square, scale=par[:, 0, p:p + 1]).then_inc(squared, 1)
                    act.activation(ks[:, :], y[:, :], ACT.Copy, scale=par[:, 0, p:p + 1]).then_inc(ks_ok, 1)
                    act.activation(kka[:, :], y[:, :], ACT.Copy, scale=par[:, 1, p:p + 1]).then_inc(kka_ok, 1)
                if kind == "r":
                    nr += 1
                    if nr > 1:
                        act.wait_ge(rrk_out, 32 * (nr - 1))
                    act.activation(rrk[:, :], y[:, :], ACT.Copy, scale=par[:, 2, p:p + 1]).then_inc(rrk_ok, 1)
                if kind == "wa":
                    act.activation(y[0:64, :], y[0:64, :], ACT.Tanh).then_inc(tanh_ok, 1)
                if kind == "gd":
                    act.activation(y[:, :], y[:, :], ACT.Sigmoid).then_inc(sig_ok, 1)
                    for q in range(4):
                        if q >= 2:
                            act.wait_ge(g_out[q % 2], 16)
                        for b in range(4):
                            act.wait_ge(g_made, 4 * q + b + 1)
                            act.activation(gate[q % 2][:, 512 * b:512 * (b + 1)], acc[:, b, :], ACT.Copy).then_inc(g_ok, 1)

        @block.tensor
        def _(pe):
            pe.wait_ge(const_in, 16 * 7)
            nk = 0
            for j, (kind, p, row, m) in enumerate(JOBS):
                y = Y[j % 2]
                if kind == "gd":
                    pe.wait_ge(sig_ok, 1)
                    for q in range(4):
                        for b in range(4):
                            if q:
                                pe.wait_ge(g_ok, 4 * (q - 1) + b + 1)
                            pe.matmul(acc[:, b, :], g2[:, q * P:(q + 1) * P], y[:, CTX + 1 + 512 * b:CTX + 1 + 512 * (b + 1)],
                                      start=True, stop=True).then_inc(g_made, 1)
                if kind == "k":
                    nk += 1
                    pe.wait_ge(squared, nk)
                    if nk == 1:
                        pe.wait_ge(g_ok, 16)
                    else:
                        pe.wait_ge(rooted, nk - 1)
                    for b, (lo, n) in enumerate(BL):
                        mm = pe.matmul(acc[:, b, 0:n], ones[:, :], norm[:, lo:lo + n], start=True, stop=True)
                    mm.then_inc(summed, 1)

        @block.gpsimd
        def _(gp):
            def store(buf, name, tile, done, rows=slice(0, P)):
                for lo, hi, d in SEGS:
                    dst = T[name][:, d:d + hi - lo] if tile is None else tiled[name][tile, :, d:d + hi - lo]
                    gp.dma_start(dst, buf[rows, lo:hi]).then_inc(done, 16)
            nk = nr = 0
            for j, (kind, p, row, m) in enumerate(JOBS):
                y = Y[j % 2]
                if j > 1 and JOBS[j - 2][0] == "k":
                    gp.wait_ge(kkn_ok, nk)
                    store(kkn, "kkn", JOBS[j - 2][1], kkn_out)
                gp.wait_ge(shifted, j + 1)
                if kind == "wa":
                    gp.wait_ge(tanh_ok, 1)
                    store(y, "waS", None, y_out[j % 2])
                if kind == "gd":
                    for q in range(4):
                        gp.wait_ge(g_ok, 4 * (q + 1))
                        gp.dma_start(tiled["gT"][q, :, :], gate[q % 2][:, 0:LAT]).then_inc(g_out[q % 2], 16)
                if kind in "krv":
                    store(y, kind + "S", p, y_out[j % 2])
                if kind == "k":
                    nk += 1
                    gp.wait_ge(kka_ok, nk)
                    store(kka, "kka", p, kka_out)
                if kind == "r":
                    nr += 1
                    gp.wait_ge(rrk_ok, nr)
                    store(rrk, "rrk", p, rrk_out)
            gp.wait_ge(kka_out, 128)
            gp.wait_ge(kkn_out, 128)
            gp.wait_ge(rrk_out, 128)
            for u in range(2):
                gp.wait_ge(g_out[u], 32)
                gp.wait_ge(y_out[u], y_stored(len(JOBS) - 2 + u))


def rwkv_chunks(nc, T):
    C = P
    NG, GH = 2, 4
    LEV = 6
    with Room(nc, "rwc") as room:
        sb, sem = room.sb, room.sem
        ident = sb("ident", [P, P])
        identb = sb("identb", [P, P], BF16)
        ident2 = sb("ident2", [P, WD])
        ones2 = sb("ones2", [P, 2])
        quad = sb("quad", [P, 2, 4, C])
        level = sb("level", [P, 2, LEV, C])
        first = sb("first", [P, 2, C])
        firstb = sb("firstb", [P, 2, C], BF16)
        scanm = sb("scanm", [P, 4, C])
        w2 = sb("w2", [P, 2, HALF])
        a2 = sb("a2", [P, 2, HALF])
        names = ("kS", "kkn", "kka", "vS", "rS", "rrk")
        ld = [{n: sb(f"{n}{d}", [P, 4, C]) for n in names} for d in range(2)]
        wS = [sb(f"wS{d}", [P, C]) for d in range(2)]
        aS = [sb(f"aS{d}", [P, C]) for d in range(2)]
        sg, L, D, D2, e_bk, e_rho, e_al, av, kd, bb, bon = [sb(n, [P, 4, C]) for n in (
            "sg", "L", "D", "D2", "e_bk", "e_rho", "e_al", "av", "kd", "bb", "bon")]
        AR = [sb(f"AR{d}", [P, 4, 4, C]) for d in range(2)]
        alpha, beta, kappa = [[sb(f"{n}{d}", [P, 4, C]) for d in range(2)] for n in ("alpha", "beta", "kappa")]
        RI = [sb(f"RI{d}", [P, 4, C + WD]) for d in range(2)]
        edge = [sb(f"edge{d}", [P, 2, 4]) for d in range(2)]
        BB = [sb(f"BB{d}", [P, WH, 2 * C + WD]) for d in range(2)]
        KK = [sb(f"KK{d}", [P, WH, 2 * C]) for d in range(2)]
        RT = [sb(f"RT{d}", [P, WH, 2 * WD]) for d in range(2)]
        kappa_t, v_t = [[sb(f"{n}{d}", [P, HALF]) for d in range(2)] for n in ("kappa_t", "v_t")]
        ATb, Tb, TTb, Xb = [sb(n, [P, NG, GH, C], BF16) for n in ("ATb", "Tb", "TTb", "Xb")]
        T32, TT32, ImT, Er, Gr = [sb(n, [P, NG, GH, C]) for n in ("T32", "TT32", "ImT", "Er", "Gr")]
        WU = sb("WU", [P, WH, 2 * WD])
        RG = sb("RG", [P, 4, C + WD])
        H = [sb(f"H{d}", [P, 4, WD]) for d in range(2)]
        Hh = sb("Hh", [P, 4, WD])
        yo = sb("yo", [P, HALF])
        bo = sb("bo", [P, 8])
        XB, TB, TTB = [[room.ps(f"{n}{g}", [P, 512]) for g in range(NG)] for n in ("XB", "TB", "TTB")]
        PB = [room.ps(f"PB{u}", [P, 512]) for u in range(2)]
        BK = [XB[0], TB[0], TTB[0], XB[1], TB[1], TTB[1]]
        f4 = lambda b: b[:, :].rearrange("p (h c) -> p h c", h=4)
        b16 = lambda b: b[:, 0:256].bitcast(BF16).rearrange("p (h c) -> p h c", h=4)

        const_in, const_ok, spent = sem("const_in"), sem("const_ok"), sem("spent")
        lds = [sem(f"lds{d}") for d in range(2)]
        N = dict(m1=8, xm=12, tm=12, ttm=10, t0m=2, t7m=2, em=2, hm=6, bvm=2, wum=2, gmm=2, ym=2, hnm=2,
                 um=1, am=1, trm=4, bonm=1,
                 m1d=8, tt0a=2, tt0=2, xd=12, td=12, ed=2, hd=6, rgd=2, hd2=2, hhat=1,
                 scan=1, dd=1, dd2=1, kd1=1, kd2=1, bd=1, betad=1, kappad=1,
                 atb=2, t0c=2, ttc=10, tt7=2, bvc=2, wuc=2, yc=2, sgu=1, asg=1, ebk=1, erho=1, eal=1, edg=2,
                 trc=4, bonc=1, t32=2, imt=2, al=1, al2=2, rho=1, rho2=2, bonp=1)
        S = {n: sem(n) for n in N}
        y_out, b_out = sem("y_out"), sem("b_out")
        block = room.block()
        NLD = 8

        def halves(eng, prologue, body):
            prologue(lambda name, k=0, ahead=0: N[name] * ahead + k)
            with eng.Fori(0, NT) as i:
                for d in range(2):
                    body(i, d, lambda name, k=0, ahead=0, d=d: i * (2 * N[name]) + ((d + ahead) * N[name] + k))

        @block.sync
        def _(sp):
            sp.dma_start(ident[:, :], T["ident"]).then_inc(const_in, 16)
            sp.dma_start(ident2[:, :], T["ident2"]).then_inc(const_in, 16)
            sp.dma_start(ones2[:, :], T["head_ones2"]).then_inc(const_in, 16)
            sp.dma_start(quad[:, :, :, :], T["quad"]).then_inc(const_in, 16)
            sp.dma_start(level[:, :, :, :], T["level"]).then_inc(const_in, 16)
            sp.dma_start(first[:, :, :], T["first"]).then_inc(const_in, 16)
            sp.dma_start(scanm[:, :, :], T["scanm"]).then_inc(const_in, 16)
            sp.wait_ge(const_ok, 2 + START)
            for d in range(2):
                for t, m, b in ((w2, "rwkv_w2", "rwkv_w0"), (a2, "rwkv_a2", "rwkv_a0")):
                    sp.dma_start(t[0:64, d, :], T[m][0, d]).then_inc(const_in, 16)
                    sp.dma_start(t[64:65, d, :], T[b][0, d:d + 1, :]).then_inc(const_in, 16)

            def load(d, at):
                for n in names:
                    sp.dma_start(ld[d][n][:, :, :], T[n][:, ds(at, C)].rearrange("(q p) t -> p q t", p=P)).then_inc(lds[d], 16)
                sp.dma_start(wS[d][0:64, :], T["waS"][0:64, ds(at, C)]).then_inc(lds[d], 16)
                sp.dma_start(aS[d][0:64, :], T["waS"][64:128, ds(at, C)]).then_inc(lds[d], 16)

            READERS = (("am", 1), ("kd2", 1), ("bd", 1), ("al", 1), ("rho", 1), ("bonp", 1), ("trm", 4))

            def used(at):
                for n, count in at:
                    sp.wait_ge(S[n], count)

            def prologue(at):
                load(0, 0)
                load(1, C)
                used([(n, at(n, k) + START) for n, k in READERS])
                load(0, C)
                sp.wait_ge(S["bonc"], 1 + START)
                sp.dma_start(T["bonus"][0, 0:C, :], bo[:, :]).then_inc(b_out, 16)

            def body(i, d, at):
                here = sp.snap(i * C if d == 0 else ((i * -1 + (NT + 1)) % NT) * C)
                soon = sp.snap(((i * -1 + (NT + 1)) % NT) * C if d == 0 else ((i + 1) % NT) * C)
                later = sp.snap(((i * -1 + NT) % NT) * C if d == 0 else ((i + 2) % NT) * C)
                counts = [(n, sp.snap(at(n, k, 1) + START)) for n, k in READERS]
                for reader in counts:
                    used([reader])
                    sp.sem_inc(spent, 1)
                load(1 - d, later)
                sp.wait_ge(S["bonc"], at("bonc", 1, 1) + START)
                sp.sem_inc(spent, 1)
                sp.dma_start(T["bonus"][1 - d, ds(soon, C), :], bo[:, :]).then_inc(b_out, 16)
                sp.wait_ge(S["yc"], at("yc", 2) + START)
                sp.sem_inc(spent, 1)
                sp.dma_start(T["y"][d, ds(here, C), :], yo[:, :]).then_inc(y_out, 16)
            halves(sp, prologue, body)
            sp.wait_ge(y_out, 16 * 2 * NT + START)
            sp.wait_ge(b_out, 16 * (2 * NT + 1) + START)
            for d in range(2):
                sp.wait_ge(lds[d], 16 * NLD * (NT + 1 + (d == 0)) + START)

        @block.gpsimd
        def _(gp):
            for d in range(2):
                gp.memset(w2[:, d, :], 0.0)
                gp.memset(a2[:, d, :], 0.0)
                for t in (wS, aS):
                    gp.memset(t[d][:, :], 0.0)
            gp.drain()
            for t in wS + aS:
                gp.memset(t[64:65, :], 1.0)
            gp.drain()
            gp.sem_inc(const_ok, 1)
            for d in range(2):
                gp.memset(AR[d][:, :, :, :], 0.0)
                gp.memset(H[d][:, :, :], 0.0)
            gp.drain()
            gp.sem_inc(const_ok, 1)
            gp.wait_ge(const_in, 16 * 15 + START)

            def prep(d, at, ahead):
                tt = gp.tensor_tensor
                gp.wait_ge(S["eal"], at("eal", 1, ahead) + START)
                tt(alpha[d][:, :, :], ld[d]["kkn"][:, :, :], e_al[:, :, :], ALU.mult).then_inc(S["al"], 1)
                gp.wait_ge(S["erho"], at("erho", 1, ahead) + START)
                tt(RI[d][:, :, 0:C], ld[d]["rS"][:, :, :], e_rho[:, :, :], ALU.mult).then_inc(S["rho"], 1)
                gp.wait_ge(S["kd2"], at("kd2", 1, ahead) + START)
                gp.wait_ge(S["bonm"], at("bonm", 0, ahead) + START)
                tt(bon[:, :, :], ld[d]["rrk"][:, :, :], kd[:, :, :], ALU.mult).then_inc(S["bonp"], 1)

            def body(i, d, at):
                for g in range(NG):
                    gp.wait_ge(S["td"], at("td", 11 + g) + START)
                    gp.tensor_tensor(ImT[:, g, :, :], ident[:, None, :].to_broadcast([P, GH, C]), Tb[:, g, :, :],
                                     ALU.subtract).then_inc(S["imt"], 1)
                prep(1 - d, at, 1)

            def prologue(at):
                prep(0, at, 0)
            halves(gp, prologue, body)

        @block.scalar
        def _(act):
            cp = lambda out, in_, n: act.activation(out, in_, ACT.Copy).then_inc(S[n], 1)
            act.wait_ge(const_in, 16 * 15 + START)
            act.activation(identb[:, :], ident[:, :], ACT.Copy)
            act.activation(firstb[:, :, :], first[:, :, :], ACT.Copy)
            for d in range(2):
                for q in range(4):
                    ins = act.activation(RI[d][:, q, C:], ident2[:, :], ACT.Copy)
            ins.then_inc(const_ok, 1)

            def rates(d, at, ahead):
                act.wait_ge(S["um"], at("um", 1, ahead) + START)
                act.wait_ge(S["dd2"], at("dd2", 0, ahead) + START)
                act.activation(sg[:, :, :], f4(PB[0]), ACT.Sigmoid).then_inc(S["sgu"], 1)
                act.wait_ge(S["am"], at("am", 1, ahead) + START)
                act.wait_ge(S["bd"], at("bd", 0, ahead) + START)
                act.activation(av[:, :, :], f4(PB[1]), ACT.Sigmoid).then_inc(S["asg"], 1)

            def scalings(d, at, ahead):
                act.wait_ge(S["dd2"], at("dd2", 1, ahead) + START)
                act.wait_ge(S["al"], at("al", 0, ahead) + START)
                act.wait_ge(S["rho"], at("rho", 0, ahead) + START)
                act.wait_ge(S["kappad"], at("kappad", 0, ahead) + START)
                x1, s1, x2, s2 = (D, DEC, D2, -DEC) if d == 0 else (D2, -DEC, D, DEC)
                act.activation(e_al[:, :, :], x2[:, :, :], ACT.Exp, scale=s2).then_inc(S["eal"], 1)
                act.activation(e_rho[:, :, :], x1[:, :, :], ACT.Exp, scale=-s1).then_inc(S["erho"], 1)
                act.activation(e_bk[:, :, :], x1[:, :, :], ACT.Exp, scale=s1).then_inc(S["ebk"], 1)
                act.activation(edge[d][:, d, :], L[:, :, 63], ACT.Exp, scale=-DEC).then_inc(S["edg"], 1)
                act.activation(edge[d][:, 1 - d, :], D[:, :, C - 1], ACT.Exp, scale=-DEC).then_inc(S["edg"], 1)

            def apart(d, at, ahead):
                for j, (n, src) in enumerate((("al", alpha[d][:, :, :]), ("rho", RI[d][:, :, 0:C]))):
                    act.wait_ge(S[n], at(n, 1, ahead) + START)
                    for h in range(2):
                        r = slice(64 * h, 64 * h + 64)
                        cp(AR[d][r, :, 2 * h + j, :], src[r], n + "2")

            def turned(d, at, ahead):
                dst = (RT[d][:, :, 0:WD], BB[d][:, :, 2 * C:], kappa_t[d][:, :].rearrange("p (h c) -> p h c", h=WH),
                       v_t[d][:, :].rearrange("p (h c) -> p h c", h=WH))
                for j in range(4):
                    act.wait_ge(S["trm"], at("trm", j + 1, ahead) + START)
                    cp(dst[j], PB[j % 2][:, :].rearrange("p (h c) -> p h c", h=WH), "trc")
                act.wait_ge(S["bonm"], at("bonm", 1, ahead) + START)
                act.wait_ge(b_out, at("bonc", 0, ahead) * 16 + START)
                cp(bo[:, :], PB[0][:, 0:8], "bonc")

            def prologue(at):
                rates(0, at, 0)
                scalings(0, at, 0)
                apart(0, at, 0)
                turned(0, at, 0)

            def body(i, d, at):
                for g in range(NG):
                    act.wait_ge(S["m1d"], at("m1d", 4 * g + 4) + START)
                    cp(ATb[:, g, :, :], BB[d][:, GH * g:GH * g + GH, 0:C], "atb")
                for g in range(NG):
                    act.wait_ge(S["t0m"], at("t0m", g + 1) + START)
                    cp(Tb[:, g, :, :], b16(TB[g]), "t0c")
                rates(1 - d, at, 1)
                for l in range(LEV - 1):
                    for g in range(NG):
                        act.wait_ge(S["ttm"], at("ttm", 2 * l + g + 1) + START)
                        cp(TTb[:, g, :, :], f4(TTB[g]), "ttc")
                for g in range(NG):
                    act.wait_ge(S["t7m"], at("t7m", g + 1) + START)
                    act.wait_ge(S["td"], at("td", 11 + g) + START)
                    cp(T32[:, g, :, :], Tb[:, g, :, :], "t32")
                    cp(TT32[:, g, :, :], b16(TTB[g]), "tt7")
                scalings(1 - d, at, 1)
                apart(1 - d, at, 1)
                turned(1 - d, at, 1)
                for g in range(NG):
                    act.wait_ge(S["bvm"], at("bvm", g + 1) + START)
                    cp(RT[d][:, GH * g:GH * g + GH, WD:], TB[g][:, 0:256].rearrange("p (h c) -> p h c", h=4), "bvc")
                for g in range(NG):
                    act.wait_ge(S["wum"], at("wum", g + 1) + START)
                    cp(WU[:, GH * g:GH * g + GH, :], f4(TTB[g]), "wuc")
                act.wait_ge(y_out, at("yc") * 8 + START)
                for o in range(2):
                    act.wait_ge(S["ym"], at("ym", o + 1) + START)
                    cp(yo[:, :].rearrange("p (q o c) -> p q o c", q=4, o=2)[:, :, o, :],
                       (TB[0], TTB[0])[o][:, 0:256].rearrange("p (q c) -> p q c", q=4), "yc")
            halves(act, prologue, body)

        @block.vector
        def _(ve):
            tt = ve.tensor_tensor
            ve.wait_ge(const_ok, 3 + START)

            def prep1(d, at, ahead):
                ve.wait_ge(S["sgu"], at("sgu", 1, ahead) + START)
                ve.wait_ge(S["edg"], at("edg", 0, ahead) + START)
                ve.tensor_tensor_scan(L[:, :, :].rearrange("p q t -> p (q t)"), scanm[:, :, :].rearrange("p q t -> p (q t)"),
                                      sg[:, :, :].rearrange("p q t -> p (q t)"), 0.0, ALU.mult, ALU.add).then_inc(S["scan"], 1)
                ve.wait_ge(S["asg"], at("asg", 1, ahead) + START)
                ve.wait_ge(S["bonp"], at("bonp", 0, ahead) + START)
                ve.scalar_tensor_tensor(kd[:, :, :], av[:, :, :], -1.0, ld[d]["kka"][:, :, :], ALU.add, ALU.mult).then_inc(S["kd1"], 1)

            def prep2(d, at, ahead):
                ve.wait_ge(S["scan"], at("scan", 1, ahead) + START)
                tt(D[:, :, :], L[:, :, :], L[:, :, 63:64].to_broadcast([P, 4, C]), ALU.subtract).then_inc(S["dd"], 1)
                ve.wait_ge(S["kd1"], at("kd1", 1, ahead) + START)
                tt(kd[:, :, :], kd[:, :, :], ld[d]["kS"][:, :, :], ALU.add).then_inc(S["kd2"], 1)

            def prep3(d, at, ahead):
                ve.wait_ge(S["dd"], at("dd", 1, ahead) + START)
                tt(D2[:, :, :], D[:, :, :], sg[:, :, :], ALU.subtract).then_inc(S["dd2"], 1)
                ve.scalar_tensor_tensor(bb[:, :, :], av[:, :, :], -1.0, ld[d]["kkn"][:, :, :], ALU.mult, ALU.mult).then_inc(S["bd"], 1)

            def prep4(d, at, ahead):
                ve.wait_ge(S["ebk"], at("ebk", 1, ahead) + START)
                ve.wait_ge(S["bd"], at("bd", 1, ahead) + START)
                tt(beta[d][:, :, :], bb[:, :, :], e_bk[:, :, :], ALU.mult).then_inc(S["betad"], 1)
                tt(kappa[d][:, :, :], kd[:, :, :], e_bk[:, :, :], ALU.mult).then_inc(S["kappad"], 1)

            def body(i, d, at):
                for j in range(8):
                    q, ks = j // 2, j % 2
                    ve.wait_ge(S["m1"], at("m1", j + 1) + START)
                    dst = (KK if ks else BB)[d][:, 2 * q:2 * q + 2, 0:2 * C]
                    tt(dst, BK[j % 6][:, :].rearrange("p (h c) -> p h c", h=2),
                       quad[:, d, :, :].rearrange("p (h x) c -> p h (x c)", h=2), ALU.mult).then_inc(S["m1d"], 1)
                for g in range(NG):
                    ve.wait_ge(S["atb"], at("atb", g + 1) + START)
                    tt(Xb[:, g, :, :], ATb[:, g, :, :], firstb[:, d, None, :].to_broadcast([P, GH, C]), ALU.mult).then_inc(S["tt0a"], 1)
                    ve.wait_ge(S["tt0a"], at("tt0a", g + 1) + START)
                    tt(TTb[:, g, :, :], Xb[:, g, :, :], identb[:, None, :].to_broadcast([P, GH, C]), ALU.add).then_inc(S["tt0"], 1)
                for l in range(LEV):
                    for g in range(NG):
                        ve.wait_ge(S["xm"], at("xm", 2 * l + g + 1) + START)
                        tt(Xb[:, g, :, :], f4(XB[g]), level[:, d, l, None, :].to_broadcast([P, GH, C]), ALU.mult).then_inc(S["xd"], 1)
                    for g in range(NG):
                        ve.wait_ge(S["tm"], at("tm", 2 * l + g + 1) + START)
                        tt(Tb[:, g, :, :], f4(TB[g]), Tb[:, g, :, :], ALU.add).then_inc(S["td"], 1)
                    if l in (1, 2, 3):
                        (prep1, prep2, prep3)[l - 1](1 - d, at, 1)
                for g in range(NG):
                    ve.wait_ge(S["imt"], at("imt", g + 1) + START)
                    ve.wait_ge(S["em"], at("em", g + 1) + START)
                    tt(Er[:, g, :, :], f4(XB[g]), ImT[:, g, :, :], ALU.add).then_inc(S["ed"], 1)
                prep4(1 - d, at, 1)
                for r in range(3):
                    for g in range(NG):
                        ve.wait_ge(S["hm"], at("hm", 2 * r + g + 1) + START)
                        tt(Gr[:, g, :, :], f4((TB, TTB, XB)[r][g]), TT32[:, g, :, :], ALU.add).then_inc(S["hd"], 1)
                tt(Hh[:, :, :], H[d][:, :, :], edge[d][:, 0, :, None].to_broadcast([P, 4, WD]), ALU.mult).then_inc(S["hhat"], 1)
                for g in range(NG):
                    ve.wait_ge(S["gmm"], at("gmm", g + 1) + START)
                    tt(RG[:, 2 * g:2 * g + 2, :], XB[g][:, 0:384].rearrange("p (q c) -> p q c", q=2),
                       RI[d][:, 2 * g:2 * g + 2, :], ALU.add).then_inc(S["rgd"], 1)
                for o in range(2):
                    r = slice(64 * o, 64 * o + 64)
                    ve.wait_ge(S["hnm"], at("hnm", o + 1) + START)
                    tt(H[d][r, :, :], (TB[1], TTB[1])[o][r, 0:256].rearrange("p (q c) -> p q c", q=4),
                       edge[d][r, 1, :, None].to_broadcast([64, 4, WD]), ALU.mult).then_inc(S["hd2"], 1)

            def prologue(at):
                for part in (prep1, prep2, prep3, prep4):
                    part(0, at, 0)
            halves(ve, prologue, body)

        @block.tensor
        def _(pe):
            mm = pe.matmul
            pe.wait_ge(const_in, 16 * 15 + START)
            pe.wait_ge(const_ok, 3 + START)

            def low_rank(d, at, ahead, i):
                pe.wait_ge(lds[d], i * (16 * NLD) + 16 * NLD + START)
                pe.wait_ge(S["bonc"], at("bonc", 0, ahead) + START)
                for q in range(4):
                    m = mm(f4(PB[0])[:, q, :], w2[:, d, q * P:q * P + P], wS[d][:, :], start=True, stop=True)
                m.then_inc(S["um"], 1)
                pe.wait_ge(S["trc"], at("trc", 0, ahead) + START)
                for q in range(4):
                    m = mm(f4(PB[1])[:, q, :], a2[:, d, q * P:q * P + P], aS[d][:, :], start=True, stop=True)
                m.then_inc(S["am"], 1)

            def turn(d, at, ahead):
                src = (alpha[d], beta[d], kappa[d], ld[d]["vS"])
                for j, n in enumerate(("al", "betad", "kappad", None)):
                    if n:
                        pe.wait_ge(S[n], at(n, 1, ahead) + START)
                    reader, count = (("sgu", 1), ("asg", 1), ("trc", 1), ("trc", 2))[j]
                    pe.wait_ge(S[reader], at(reader, count, ahead) + START)
                    for q in range(4):
                        m = pe.transpose(f4(PB[j % 2])[:, q, :], src[j][:, q, :], ident[:, :])
                    m.then_inc(S["trm"], 1)
                pe.wait_ge(S["trc"], at("trc", 3, ahead) + START)
                pe.wait_ge(S["bonp"], at("bonp", 1, ahead) + START)
                for q in range(4):
                    m = mm(PB[0][:, 2 * q:2 * q + 2], bon[:, q, :], ones2[:, :], start=True, stop=True)
                m.then_inc(S["bonm"], 1)

            def prologue(at):
                low_rank(0, at, 0, 0)
                turn(0, at, 0)

            def body(i, d, at):
                for n in ("rgd", "hd2", "yc", "hd", "wuc"):
                    pe.wait_ge(S[n], at(n) + START)
                pe.wait_ge(S["rho2"], at("rho2", 2) + START)
                pe.wait_ge(S["al2"], at("al2", 2) + START)
                for j in range(8):
                    q, ks = j // 2, j % 2
                    if j >= 6:
                        pe.wait_ge(S["m1d"], at("m1d", j - 5) + START)
                    mm(BK[j % 6][:, :], (kappa if ks else beta)[d][:, q, :], AR[d][:, q, :, :].rearrange("p a c -> p (a c)"),
                       start=True, stop=True).then_inc(S["m1"], 1)
                low_rank(1 - d, at, 1, i if d == 0 else i + 1)
                pe.wait_ge(S["m1d"], at("m1d", 8) + START)
                for g in range(NG):
                    pe.wait_ge(S["tt0"], at("tt0", g + 1) + START)
                    for h in range(GH):
                        m = pe.transpose(b16(TB[g])[:, h, :], TTb[:, g, h, :], identb[:, :])
                    m.then_inc(S["t0m"], 1)
                for l in range(LEV):
                    for g in range(NG):
                        if l == 0:
                            pe.wait_ge(S["t0c"], at("t0c", g + 1) + START)
                        else:
                            pe.wait_ge(S["td"], at("td", 2 * (l - 1) + g + 1) + START)
                        for h in range(GH):
                            m = mm(f4(XB[g])[:, h, :], ATb[:, g, h, :], Tb[:, g, h, :], start=True, stop=True)
                        m.then_inc(S["xm"], 1)
                    for g in range(NG):
                        pe.wait_ge(S["xd"], at("xd", 2 * l + g + 1) + START)
                        if l:
                            pe.wait_ge(S["ttc"], at("ttc", 2 * (l - 1) + g + 1) + START)
                        for h in range(GH):
                            m = mm(f4(TB[g])[:, h, :], TTb[:, g, h, :], Xb[:, g, h, :], start=True, stop=True)
                        m.then_inc(S["tm"], 1)
                        if l < LEV - 1:
                            for h in range(GH):
                                mm(f4(TTB[g])[:, h, :], Xb[:, g, h, :], TTb[:, g, h, :], start=True, stop=False)
                                m = mm(f4(TTB[g])[:, h, :], identb[:, :], TTb[:, g, h, :], start=False, stop=True)
                            m.then_inc(S["ttm"], 1)
                for g in range(NG):
                    pe.wait_ge(S["td"], at("td", 11 + g) + START)
                    for h in range(GH):
                        m = pe.transpose(b16(TTB[g])[:, h, :], Tb[:, g, h, :], identb[:, :])
                    m.then_inc(S["t7m"], 1)
                for g in range(NG):
                    pe.wait_ge(S["t32"], at("t32", g + 1) + START)
                    for h in range(GH):
                        m = mm(f4(XB[g])[:, h, :], BB[d][:, GH * g + h, 0:C], T32[:, g, h, :], start=True, stop=True)
                    m.then_inc(S["em"], 1)
                for r in range(3):
                    for g in range(NG):
                        if r == 0:
                            pe.wait_ge(S["ed"], at("ed", g + 1) + START)
                        else:
                            pe.wait_ge(S["hd"], at("hd", 2 * r - 1 + g) + START)
                        if r == 0:
                            pe.wait_ge(S["tt7"], at("tt7", g + 1) + START)
                        for h in range(GH):
                            m = mm(f4((TB, TTB, XB)[r][g])[:, h, :], Er[:, g, h, :], (Gr if r else TT32)[:, g, h, :],
                                   start=True, stop=True)
                        m.then_inc(S["hm"], 1)
                for g in range(NG):
                    pe.wait_ge(S["hd"], at("hd", 1 + g) + START)
                    for h in range(GH):
                        m = mm(TB[g][:, 64 * h:64 * h + 64], KK[d][:, GH * g + h, 0:C], v_t[d][:, (GH * g + h) * WD:(GH * g + h + 1) * WD],
                               start=True, stop=True)
                    m.then_inc(S["bvm"], 1)
                turn(1 - d, at, 1)
                for g in range(NG):
                    pe.wait_ge(S["hd"], at("hd", 5 + g) + START)
                    pe.wait_ge(S["bvc"], at("bvc", g + 1) + START)
                    for h in range(GH):
                        m = mm(f4(TTB[g])[:, h, :], Gr[:, g, h, :], RT[d][:, GH * g + h, :], start=True, stop=True)
                    m.then_inc(S["wum"], 1)
                for g in range(NG):
                    pe.wait_ge(S["wuc"], at("wuc", g + 1) + START)
                    for h in range(GH):
                        o = 64 * (h % 2)
                        m = mm(XB[g][o:o + 64, 192 * (h // 2):192 * (h // 2) + 192], WU[:, GH * g + h, 0:WD], BB[d][:, GH * g + h, C:],
                               start=True, stop=True)
                    m.then_inc(S["gmm"], 1)
                pe.wait_ge(S["hhat"], at("hhat", 1) + START)
                pe.wait_ge(S["bvc"], at("bvc", 2) + START)
                pe.wait_ge(S["rgd"], at("rgd", 2) + START)
                pe.wait_ge(S["wuc"], at("wuc", 2) + START)
                for o in range(2):
                    r, bank = slice(64 * o, 64 * o + 64), (TB[0], TTB[0])[o]
                    for q in range(4):
                        n = 2 * q + o
                        c, v = slice(WD * q, WD * q + WD), slice(WD * n, WD * n + WD)
                        mm(bank[:, c], BB[d][:, n, C:2 * C], WU[:, n, WD:], start=True, stop=False)
                        mm(bank[:, c], KK[d][:, n, C:], v_t[d][:, v], start=False, stop=False)
                        m = mm(bank[:, c], RG[r, q, 0:C], Hh[r, q, :], start=False, stop=True)
                    m.then_inc(S["ym"], 1)
                for o in range(2):
                    r, bank = slice(64 * o, 64 * o + 64), (TB[1], TTB[1])[o]
                    for q in range(4):
                        n = 2 * q + o
                        c, v = slice(WD * q, WD * q + WD), slice(WD * n, WD * n + WD)
                        mm(bank[r, c], BB[d][:, n, 2 * C:], WU[:, n, WD:], start=True, stop=False)
                        mm(bank[r, c], kappa_t[d][:, v], v_t[d][:, v], start=False, stop=False)
                        m = mm(bank[r, c], RG[r, q, C:], Hh[r, q, :], start=False, stop=True)
                    m.then_inc(S["hnm"], 1)
            halves(pe, prologue, body)


def rotate(nc, T):
    with Room(nc, "rot") as room:
        sb, sem = room.sb, room.sem
        cos, sin = sb("cos", [P, LAT]), sb("sin", [P, LAT])
        x = [[sb(f"x{u}{h}", [P, TOK]) for h in range(2)] for u in range(2)]
        a, b = sb("a", [P, LAT]), sb("b", [P, LAT])
        c, e = sb("c", [P, LAT]), sb("e", [P, LAT])
        o = [[sb(f"o{u}{h}", [P, TOK]) for h in range(2)] for u in range(2)]
        const_in, fa, fb, fo, zero = sem("const_in"), sem("fa"), sem("fb"), sem("fo"), sem("zero")
        fc, fe, ctx_ok, ctx_free = sem("fc"), sem("fe"), sem("ctx_ok"), sem("ctx_free")
        x_in = [sem(f"x_in{u}") for u in range(2)]
        out = [sem(f"out{u}") for u in range(2)]
        zT = T["zT"].rearrange("(n p) t -> n p t", p=P)
        JOBS = [("kTr", Z_RK + 2 * q, q, RD ** -0.5, 0) for q in range(2)] + [("qTr", Z_RQ + 2 * q, q, 1.0, CTX) for q in range(2)]
        block = room.block()

        @block.sync
        def _(sp):
            sp.dma_start(cos[:, :], T["cosT"]).then_inc(const_in, 16)
            sp.dma_start(sin[:, :], T["sinT"]).then_inc(const_in, 16)
            for j, (name, row, q, s, lo) in enumerate(JOBS):
                if j >= 2:
                    sp.wait_ge(fe, j - 1 + START)
                    sp.wait_ge(fb, j - 1 + START)
                    sp.wait_ge(ctx_ok, j - 1 + START)
                for h in range(2):
                    sp.dma_start(x[j % 2][h][:, lo:], zT[row + h, :, lo:]).then_inc(x_in[j % 2], 16)

        @block.vector
        def _(ve):
            ve.wait_ge(const_in, 32 + START)
            for j, (name, row, q, s, lo) in enumerate(JOBS):
                x1, x2 = x[j % 2]
                ve.wait_ge(x_in[j % 2], 32 * (j // 2 + 1) + START)
                ve.scalar_tensor_tensor(a[:, :], x1[:, CTX:], s, cos[:, :], ALU.mult, ALU.mult).then_inc(fa, 1)
                ve.scalar_tensor_tensor(b[:, :], x2[:, CTX:], s, sin[:, :], ALU.mult, ALU.mult).then_inc(fb, 1)
                if j >= 2:
                    ve.wait_ge(out[j % 2], 64 * (j // 2) + START)
                ve.wait_ge(fb, j + 1 + START)
                ve.tensor_tensor(o[j % 2][0][:, CTX:], a[:, :], b[:, :], ALU.subtract).then_inc(fo, 1)
                ve.scalar_tensor_tensor(c[:, :], x1[:, CTX:], s, sin[:, :], ALU.mult, ALU.mult).then_inc(fc, 1)
                ve.scalar_tensor_tensor(e[:, :], x2[:, CTX:], s, cos[:, :], ALU.mult, ALU.mult).then_inc(fe, 1)
                ve.wait_ge(fe, j + 1 + START)
                ve.tensor_tensor(o[j % 2][1][:, CTX:], c[:, :], e[:, :], ALU.add).then_inc(fo, 1)

        @block.scalar
        def _(act):
            for j, (name, row, q, s, lo) in enumerate(JOBS):
                act.wait_ge(x_in[j % 2], 32 * (j // 2 + 1) + START)
                if j >= 2:
                    act.wait_ge(out[j % 2], 64 * (j // 2) + START)
                for h in range(2):
                    if name == "kTr":
                        ins = act.activation(o[j % 2][h][:, 0:CTX], x[j % 2][h][:, 0:CTX], ACT.Copy, scale=s)
                    else:
                        ins = act.activation(o[j % 2][h][:, 0:CTX], cos[:, 0:CTX], ACT.Copy, scale=0.0)
                ins.then_inc(ctx_ok, 1)
                act.wait_ge(ctx_ok, j + 1 + START)
                act.wait_ge(fo, 2 * j + 2 + START)
                for h in range(2):
                    for k in range(2):
                        r = slice(64 * k, 64 * k + 64)
                        at = (2 * q + k) * RD + 64 * h
                        act.dma_start(T[name][at:at + 64, :], o[j % 2][h][r, :]).then_inc(out[j % 2], 16)
            for u in range(2):
                act.wait_ge(out[u], 32 * len(JOBS) + START)


def rows_of(t, at):
    return t[:, ds(at, P)].rearrange("(q p) t -> p q t", p=P)


def decay_logs(act, lg, lgr, done):
    act.activation(lgr[:, :], lgr[:, :], ACT.Exp).then_inc(done, 1)
    act.wait_ge(done, 1 + START)
    act.activation(lg[:, :], lgr[:, :], ACT.Copy, scale=-1.0).then_inc(done, 1)
    act.wait_ge(done, 2 + START)


def retention_backward(nc, T):
    C = P
    with Room(nc, "rtb") as room:
        sb, sem = room.sb, room.sem
        ident = sb("ident", [P, P])
        lgr, lg, whole, tpos, tail = sb("lgr", [P, 8]), sb("lg", [P, 8]), sb("whole", [P, 8]), sb("tpos", [P, 2]), sb("tail", [P, RH])
        kT, vT, R = [[sb(f"{n}{u}", [P, RH, C]) for u in range(2)] for n in ("kT", "vT", "R")]
        kt, vt = sb("kt", [P, RH, C]), sb("vt", [P, RH, C])
        kp, vp, rp = [room.ps(n, [P, RH, C]) for n in ("kp", "vp", "rp")]
        spent, const_in, setup, zeroed = sem("spent"), sem("const_in"), sem("setup"), sem("zeroed")
        rows_in = [sem(f"rows_in{u}") for u in range(2)]
        k_turned, v_turned, kt_ok, vt_ok, made, R_ok = [sem(n) for n in ("k_turned", "v_turned", "kt_ok", "vt_ok", "made", "R_ok")]
        stored = [sem(f"stored{u}") for u in range(2)]
        zv = T["zT"][Z_RV * P:(Z_RV + 4) * P, :]
        block = room.block()

        @block.sync
        def _(sp):
            sp.dma_start(ident[:, :], T["ident"]).then_inc(const_in, 16)
            sp.dma_start(tpos[:, :], T["tail_pos"]).then_inc(const_in, 16)
            sp.dma_start(lgr[:, :], T["ret_log_decay"].rearrange("a d h -> a (d h)").to_broadcast([P, 8])).then_inc(const_in, 16)

            def load(u, at):
                sp.dma_start(kT[u][:, :, :], rows_of(T["kTr"], at)).then_inc(rows_in[u], 16)
                sp.dma_start(vT[u][:, :, :], rows_of(zv, at)).then_inc(rows_in[u], 16)
            load(0, C)
            load(1, 0)
            sp.wait_ge(zeroed, 2 + START)
            with sp.Fori(0, NT // 2) as i:
                for u in range(2):
                    at = sp.snap(((i * -2 + (2 * NT - 1 - u)) % NT) * C)
                    chunk = sp.snap((i * -2 + (NT + 1 - u)) % NT)
                    sp.wait_ge(R_ok, (i * 2 + u) * RH + START)
                    sp.sem_inc(spent, 1)
                    sp.dma_start(T["Rb"][ds(chunk, 1), :, :, :], R[u][:, :, :]).then_inc(stored[u], 16)
                    sp.wait_ge(v_turned, i * 2 + (u + 1) + START)
                    sp.sem_inc(spent, 1)
                    load(u, at)
            for u in range(2):
                sp.wait_ge(stored[u], 8 * NT + START)
            for u in range(2):
                sp.wait_ge(rows_in[u], 32 * (NT // 2 + 1) + START)

        @block.scalar
        def _(act):
            act.wait_ge(const_in, 48 + START)
            decay_logs(act, lg, lgr, setup)
            for h in range(RH):
                act.activation(tail[:, h:h + 1], tpos[:, 1:2], ACT.Exp, scale=lg[:, RH + h:RH + h + 1])
            act.activation(whole[:, :], lg[:, :], ACT.Exp, scale=float(C)).then_inc(setup, 1)
            with act.Fori(0, NT // 2) as i:
                for u in range(2):
                    act.wait_ge(v_turned, i * 2 + (u + 1) + START)
                    act.wait_ge(made, i * 2 + u + START)
                    act.activation(vt[:, :, :], vp[:, :, :], ACT.Copy).then_inc(vt_ok, 1)

        @block.vector
        def _(ve):
            for r in R:
                ve.memset(r[:, :, :], 0.0).then_inc(zeroed, 1)
            ve.wait_ge(setup, 3 + START)
            ve.wait_ge(zeroed, 2 + START)
            with ve.Fori(0, NT // 2) as i:
                for u in range(2):
                    ve.wait_ge(k_turned, i * 2 + (u + 1) + START)
                    ve.wait_ge(made, i * 2 + u + START)
                    ve.tensor_tensor(kt[:, :, :], kp[:, :, :], tail[:, :, None].to_broadcast([P, RH, C]), ALU.mult).then_inc(kt_ok, 1)
                    ve.wait_ge(made, i * 2 + (u + 1) + START)
                    ve.wait_ge(stored[1 - u], i * 16 + 16 * u + START)
                    ve.wait_ge(R_ok, (i * 2 + u) * RH + START)
                    for h in range(RH):
                        ve.scalar_tensor_tensor(R[1 - u][:, h, :], R[u][:, h, :], whole[:, RH + h:RH + h + 1], rp[:, h, :],
                                                ALU.mult, ALU.add).then_inc(R_ok, 1)

        @block.tensor
        def _(pe):
            pe.wait_ge(const_in, 48 + START)
            with pe.Fori(0, NT // 2) as i:
                for u in range(2):
                    pe.wait_ge(rows_in[u], i * 32 + 32 + START)
                    pe.wait_ge(kt_ok, i * 2 + u + START)
                    pe.wait_ge(vt_ok, i * 2 + u + START)
                    for h in range(RH):
                        t = pe.transpose(kp[:, h, :], kT[u][:, h, :], ident[:, :])
                    t.then_inc(k_turned, 1)
                    for h in range(RH):
                        t = pe.transpose(vp[:, h, :], vT[u][:, h, :], ident[:, :])
                    t.then_inc(v_turned, 1)
                    pe.wait_ge(kt_ok, i * 2 + (u + 1) + START)
                    pe.wait_ge(vt_ok, i * 2 + (u + 1) + START)
                    pe.wait_ge(R_ok, (i * 2 + u) * RH + START)
                    for h in range(RH):
                        m = pe.matmul(rp[:, h, :], kt[:, h, :], vt[:, h, :], start=True, stop=True)
                    m.then_inc(made, 1)



def retention_forward(nc, T):
    C = P
    with Room(nc, "rtf") as room:
        sb, sem = room.sb, room.sem
        ident = sb("ident", [P, P])
        lgr, lg, whole, tpos, tail = sb("lgr", [P, 8]), sb("lg", [P, 8]), sb("whole", [P, 8]), sb("tpos", [P, 2]), sb("tail", [P, RH])
        rel = sb("rel", [P, 6, C])
        tab = sb("tab", [P, 2, RH, C])
        dk = sb("dk", [P, RH, C])
        cross = [sb(f"cross{d}", [P, RH, C]) for d in range(2)]
        gn, eps = sb("gn", [P, 4]), sb("eps", [P, 1])
        kT, vT, qT, gT, Rb, R, yr = [[sb(f"{n}{u}", [P, RH, C]) for u in range(2)] for n in ("kT", "vT", "qT", "gT", "Rb", "R", "yr")]
        kt, vt, qf, qb, Sm, on = [sb(n, [P, RH, C]) for n in ("kt", "vt", "qf", "qb", "Sm", "on")]
        st6, mv, sd, rs = sb("st6", [P, RH, 6]), sb("mv", [P, RH, 2]), sb("sd", [P, RH]), sb("rs", [P, RH])
        kp, vp, s_p, o_p, rp, tp = [room.ps(n, [P, RH, C]) for n in ("kp", "vp", "s_p", "o_p", "rp", "tp")]
        spent, stats, const_in, setup, table, ready = sem("spent"), sem("stats"), sem("const_in"), sem("setup"), sem("table"), sem("ready")
        rows_in, y_out = [[sem(f"{n}{u}") for u in range(2)] for n in ("rows_in", "y_out")]
        (k_turned, v_turned, kt_ok, vt_ok, made, R_ok, s_made, s_ok, qf_ok, qb_ok, o_made, bn, aggr, rooted, rec,
         on_ok, o_turned, y_ok) = [sem(n) for n in (
             "k_turned", "v_turned", "kt_ok", "vt_ok", "made", "R_ok", "s_made", "s_ok", "qf_ok", "qb_ok", "o_made",
             "bn", "aggr", "rooted", "rec", "on_ok", "o_turned", "y_ok")]
        zv = T["zT"][Z_RV * P:(Z_RV + 4) * P, :]
        zg = T["zT"][Z_RG * P:(Z_RG + 4) * P, :]
        yT = T["yrT"]
        NL = LAT // C
        block = room.block()

        def chunks(eng, body):
            for u in range(2):
                body(u, None, u)
            for u in range(2):
                body(u, u, u + 2)
            with eng.Fori(1, NL // 2) as i:
                for u in range(2):
                    body(u, i * 2 + u, i * 2 + (u + 2))

        @block.sync
        def _(sp):
            sp.dma_start(ident[:, :], T["ident"]).then_inc(const_in, 16)
            sp.dma_start(tpos[:, :], T["tail_pos"]).then_inc(const_in, 16)
            sp.dma_start(rel[:, :, :], T["rel"]).then_inc(const_in, 16)
            sp.dma_start(lgr[:, :], T["ret_log_decay"].rearrange("a d h -> a (d h)").to_broadcast([P, 8])).then_inc(const_in, 16)
            with nc.allow_non_contiguous_dma("channel parameters over partitions"):
                sp.dma_start(gn[:, :], T["ret_gn_g"].rearrange("a (t p) -> p (a t)", p=P)).then_inc(const_in, 16)

            def load_state(u, at):
                sp.dma_start(kT[u][:, :, :], rows_of(T["kTr"], at)).then_inc(rows_in[u], 16)
                sp.dma_start(vT[u][:, :, :], rows_of(zv, at)).then_inc(rows_in[u], 16)

            def load_gate(u, at):
                sp.dma_start(gT[u][:, :, :], rows_of(zg, at)).then_inc(rows_in[u], 16)

            def load(u, at, chunk):
                load_state(u, at)
                sp.dma_start(qT[u][:, :, :], rows_of(T["qTr"], at)).then_inc(rows_in[u], 16)
                sp.dma_start(Rb[u][:, :, :], T["Rb"][ds(chunk, 1), :, :, :]).then_inc(rows_in[u], 16)
            for u in range(2):
                load_state(u, u * C)
            for u in range(2):
                sp.wait_ge(v_turned, u + 1 + START)
                load(u, CTX + u * C, CT + u)
                load_gate(u, CTX + u * C)
            with sp.Fori(0, NL // 2 - 1) as i:
                for u in range(2):
                    at, chunk = sp.snap(i * (2 * C) + (CTX + (2 + u) * C)), sp.snap(i * 2 + (CT + 2 + u))
                    count = sp.snap(i * 2 + (u + 1) + START)
                    here = sp.snap(i * (2 * C) + u * C)
                    state_count = sp.snap(i * 2 + (u + 3) + START)
                    sp.wait_ge(o_made, count)
                    sp.sem_inc(spent, 1)
                    sp.wait_ge(v_turned, state_count)
                    sp.sem_inc(spent, 1)
                    load(u, at, chunk)
                    sp.wait_ge(y_ok, count)
                    sp.sem_inc(spent, 1)
                    sp.dma_start(rows_of(yT, here), yr[u][:, :, :]).then_inc(y_out[u], 16)
                    load_gate(u, at)
            for u in range(2):
                sp.wait_ge(y_ok, NL - 1 + u + START)
                sp.dma_start(rows_of(yT, LAT + (u - 2) * C), yr[u][:, :, :]).then_inc(y_out[u], 16)
            for u in range(2):
                sp.wait_ge(y_out[u], 8 * NL + START)

        @block.scalar
        def _(act):
            act.wait_ge(const_in, 80 + START)
            decay_logs(act, lg, lgr, setup)
            for h in range(RH):
                act.activation(tail[:, h:h + 1], tpos[:, 0:1], ACT.Exp, scale=lg[:, h:h + 1])
                for d in range(2):
                    g = lg[:, RH * d + h:RH * d + h + 1]
                    act.activation(tab[:, d, h, :], rel[:, d, :], ACT.Exp, scale=g)
                    act.activation(cross[d][:, h, :], rel[:, 4 + d, :], ACT.Exp, scale=g)
            act.activation(whole[:, :], lg[:, :], ACT.Exp, scale=float(C)).then_inc(setup, 1)

            def body(u, f, s):
                act.wait_ge(v_turned, s + 1 + START)
                act.wait_ge(made, s + START)
                act.activation(vt[:, :, :], vp[:, :, :], ACT.Copy).then_inc(vt_ok, 1)
                if f is not None:
                    act.wait_ge(aggr, f * RH + RH + START)
                    act.wait_ge(rec, f + START)
                    act.activation(sd[:, :], mv[:, :, 1], ACT.Sqrt, bias=eps[:, :]).then_inc(rooted, 1)
            act.wait_ge(ready, 1 + START)
            chunks(act, body)

        @block.gpsimd
        def _(gp):
            gp.wait_ge(setup, 3 + START)

            with gp.Fori(0, NL // 2) as i:
                for u in range(2):
                    gp.wait_ge(rows_in[u], i * 80 + 112 + START)
                    gp.wait_ge(o_made, i * 2 + u + START)
                    gp.tensor_tensor(qf[:, :, :], qT[u][:, :, :], cross[0][:, :, :], ALU.mult).then_inc(qf_ok, 1)
                    gp.tensor_tensor(qb[:, :, :], qT[u][:, :, :], cross[1][:, :, :], ALU.mult).then_inc(qb_ok, 1)

        @block.vector
        def _(ve):
            tt = ve.tensor_tensor
            ve.memset(eps[:, :], RET_EPS)
            ve.memset(R[0][:, :, :], 0.0).then_inc(table, 1)
            ve.wait_ge(table, 1 + START)
            ve.wait_ge(setup, 3 + START)
            tt(tab[:, 0, :, :], tab[:, 0, :, :], rel[:, 2, None, :].to_broadcast([P, RH, C]), ALU.mult).then_inc(table, 1)
            tt(tab[:, 1, :, :], tab[:, 1, :, :], rel[:, 3, None, :].to_broadcast([P, RH, C]), ALU.mult).then_inc(table, 1)
            ve.wait_ge(table, 3 + START)
            tt(dk[:, :, :], tab[:, 0, :, :], tab[:, 1, :, :], ALU.add).then_inc(table, 1)
            ve.wait_ge(table, 4 + START)
            ve.sem_inc(ready, 1)

            def body(u, f, s):
                ve.wait_ge(k_turned, s + 1 + START)
                ve.wait_ge(made, s + START)
                tt(kt[:, :, :], kp[:, :, :], tail[:, :, None].to_broadcast([P, RH, C]), ALU.mult).then_inc(kt_ok, 1)
                if f is not None:
                    ve.wait_ge(s_made, f + 1 + START)
                    ve.wait_ge(o_made, f + START)
                    tt(Sm[:, :, :], s_p[:, :, :], dk[:, :, :], ALU.mult).then_inc(s_ok, 1)
                ve.wait_ge(made, s + 1 + START)
                ve.wait_ge(R_ok, s * RH + START)
                if f is not None:
                    ve.wait_ge(o_made, f + START)
                for h in range(RH):
                    ve.scalar_tensor_tensor(R[1 - u][:, h, :], R[u][:, h, :], whole[:, h:h + 1], rp[:, h, :],
                                            ALU.mult, ALU.add).then_inc(R_ok, 1)
                if f is None:
                    return
                if not (isinstance(s, int) and s == 2):
                    gate(1 - u, f - 1)
                ve.wait_ge(o_made, f + 1 + START)
                for h in range(RH):
                    ve.bn_stats(st6[:, h, :], o_p[:, h, :]).then_inc(bn, 1)
                ve.wait_ge(bn, f * RH + RH + START)
                ve.sem_inc(stats, 1)
                for h in range(RH):
                    ve.bn_aggr(mv[:, h, :], st6[:, h, :]).then_inc(aggr, 1)
                ve.wait_ge(rooted, f + 1 + START)
                ve.reciprocal(rs[:, :], sd[:, :]).then_inc(rec, 1)
                ve.wait_ge(rec, f + 1 + START)
                ve.wait_ge(o_turned, f + START)
                for h in range(RH):
                    ins = ve.tensor_scalar(on[:, h, :], o_p[:, h, :], mv[:, h, 0:1], rs[:, h:h + 1], ALU.subtract, ALU.mult)
                ins.then_inc(on_ok, 1)

            def gate(u, f):
                ve.wait_ge(o_turned, f + 1 + START)
                ve.wait_ge(y_out[u], (f - u) * 8 + START)
                for h in range(RH):
                    ins = ve.scalar_tensor_tensor(yr[u][:, h, :], tp[:, h, :], gn[:, h:h + 1], gT[u][:, h, :], ALU.mult, ALU.mult)
                ins.then_inc(y_ok, 1)
            chunks(ve, body)
            gate(1, NL - 1)

        @block.tensor
        def _(pe):
            pe.wait_ge(ready, 1 + START)

            def body(u, f, s):
                pe.wait_ge(rows_in[u], (32 if f is None else (f - u) * 40 + 112) + START)
                pe.wait_ge(kt_ok, s + START)
                pe.wait_ge(vt_ok, s + START)
                for h in range(RH):
                    t = pe.transpose(kp[:, h, :], kT[u][:, h, :], ident[:, :])
                t.then_inc(k_turned, 1)
                for h in range(RH):
                    t = pe.transpose(vp[:, h, :], vT[u][:, h, :], ident[:, :])
                t.then_inc(v_turned, 1)
                if f is not None:
                    pe.wait_ge(s_ok, f + START)
                    for h in range(RH):
                        m = pe.matmul(s_p[:, h, :], kT[u][:, h, :], qT[u][:, h, :], start=True, stop=True)
                    m.then_inc(s_made, 1)
                    if not (isinstance(s, int) and s == 2):
                        turn(f - 1)
                pe.wait_ge(kt_ok, s + 1 + START)
                pe.wait_ge(vt_ok, s + 1 + START)
                pe.wait_ge(R_ok, s * RH + START)
                for h in range(RH):
                    m = pe.matmul(rp[:, h, :], kt[:, h, :], vt[:, h, :], start=True, stop=True)
                m.then_inc(made, 1)
                if f is None:
                    return
                pe.wait_ge(s_ok, f + 1 + START)
                pe.wait_ge(qf_ok, f + 1 + START)
                pe.wait_ge(qb_ok, f + 1 + START)
                pe.wait_ge(on_ok, f + START)
                for h in range(RH):
                    pe.matmul(o_p[:, h, :], Sm[:, h, :], vt[:, h, :], start=True, stop=False)
                    pe.matmul(o_p[:, h, :], qf[:, h, :], R[u][:, h, :], start=False, stop=False)
                    m = pe.matmul(o_p[:, h, :], qb[:, h, :], Rb[u][:, h, :], start=False, stop=True)
                m.then_inc(o_made, 1)

            def turn(f):
                pe.wait_ge(on_ok, f + 1 + START)
                pe.wait_ge(y_ok, f + START)
                for h in range(RH):
                    t = pe.transpose(tp[:, h, :], on[:, h, :], ident[:, :])
                t.then_inc(o_turned, 1)
            chunks(pe, body)
            turn(NL - 1)


def rwkv_output(nc, T):
    NL, B = LAT // P, 4
    with Room(nc, "rwo") as room:
        sb, sem = room.sb, room.sem
        ident, ln, eps = sb("ident", [P, P]), sb("ln", [P, 2, 4]), sb("eps", [P, 1])
        y, v, g, w = [[sb(f"{n}{u}", s) for u in range(B)] for n, s in (
            ("y", [P, 2, HALF]), ("v", [P, 4, P]), ("g", [P, 4, P]), ("w", [P, 4, P]))]
        b = [sb(f"b{u}", [P, 2, WH]) for u in range(B)]
        be = [sb(f"be{u}", [P, HALF]) for u in range(B)]
        ys, yn = sb("ys", [P, HALF]), [sb(f"yn{u}", [P, HALF]) for u in range(B)]
        yc = sb("yc", [P, HALF])
        st6, mv, sd, rs = sb("st6", [P, WH, 6]), sb("mv", [P, WH, 2]), sb("sd", [P, WH]), sb("rs", [P, WH])
        wn, wb, wg = sb("wn", [P, 4, P]), sb("wb", [P, 4, P]), sb("wg", [P, 4, P])
        yp, bp = [[room.ps(f"{n}{u}", [P, 4, P]) for u in range(B)] for n in ("yp", "bp")]
        rows_in, w_out = [[sem(f"{n}{u}") for u in range(B)] for n in ("rows_in", "w_out")]
        (const_in, spent, be_ok, ys_ok, bn, stats, aggr, rooted, rec, yc_ok, yn_ok, y_turned, b_turned, wn_ok, wb_ok,
         wg_ok, w_ok) = [sem(n) for n in ("const_in", "spent", "be_ok", "ys_ok", "bn", "stats", "aggr", "rooted", "rec",
                                          "yc_ok", "yn_ok", "y_turned", "b_turned", "wn_ok", "wb_ok", "wg_ok", "w_ok")]
        block = room.block()

        @block.sync
        def _(sp):
            sp.dma_start(ident[:, :], T["ident"]).then_inc(const_in, 16)
            with nc.allow_non_contiguous_dma("channel parameters over partitions"):
                for j, n in enumerate(("rwkv_ln_g", "rwkv_ln_b")):
                    sp.dma_start(ln[:, j, :], T[n].rearrange("a (t p) -> p (a t)", p=P)).then_inc(const_in, 16)

            def load(u, at, lat):
                for d in range(2):
                    sp.dma_start(y[u][:, d, :], T["y"][d, ds(at, P), :]).then_inc(rows_in[u], 16)
                    sp.dma_start(b[u][:, d, :], T["bonus"][d, ds(at, P), :]).then_inc(rows_in[u], 16)
                sp.dma_start(v[u][:, :, :], rows_of(T["vS"], at)).then_inc(rows_in[u], 16)
                sp.dma_start(g[u][:, :, :], rows_of(T["gT"], lat)).then_inc(rows_in[u], 16)
            for u in range(B):
                load(u, CTX + u * P, u * P)
            with sp.Fori(0, NL // B - 1) as i:
                for u in range(B):
                    at, lat = sp.snap(i * (B * P) + (CTX + (B + u) * P)), sp.snap(i * (B * P) + (B + u) * P)
                    here = sp.snap(i * (B * P) + u * P)
                    sp.wait_ge(w_ok, sp.snap(i * B + (u + 1) + START))
                    sp.sem_inc(spent, 1)
                    sp.dma_start(rows_of(T["ywT"], here), w[u][:, :, :]).then_inc(w_out[u], 16)
                    load(u, at, lat)
            for u in range(B):
                sp.wait_ge(w_ok, NL - B + 1 + u + START)
                sp.dma_start(rows_of(T["ywT"], LAT + (u - B) * P), w[u][:, :, :]).then_inc(w_out[u], 16)
            for u in range(B):
                sp.wait_ge(w_out[u], 16 * (NL // B) + START)

        @block.gpsimd
        def _(gp):
            gp.wait_ge(const_in, 48 + START)
            with gp.Fori(0, NL // B) as i:
                for u in range(B):
                    gp.wait_ge(rows_in[u], i * 96 + 96 + START)
                    gp.wait_ge(b_turned, i * B + START)
                    gp.tensor_tensor(be[u][:, :].rearrange("p (h c) -> p h c", h=WH), b[u][:, 0, :, None].to_broadcast([P, WH, WD]),
                                     b[u][:, 1, :, None].to_broadcast([P, WH, WD]), ALU.add).then_inc(be_ok, 1)
                    gp.wait_ge(wn_ok, i * B + (u + 1) + START)
                    gp.wait_ge(wb_ok, i * B + (u + 1) + START)
                    gp.tensor_tensor(wg[:, :, :], wn[:, :, :], wb[:, :, :], ALU.add).then_inc(wg_ok, 1)
                    gp.wait_ge(wg_ok, i * B + (u + 1) + START)
                    gp.wait_ge(w_out[u], i * 16 + START)
                    gp.tensor_tensor(w[u][:, :, :], wg[:, :, :], g[u][:, :, :], ALU.mult).then_inc(w_ok, 1)

        @block.vector
        def _(ve):
            heads = lambda t: t[:, :].rearrange("p (h c) -> p h c", h=WH)
            wide = lambda t: t.to_broadcast([P, WH, WD])
            ve.memset(eps[:, :], RWKV_EPS).then_inc(rec, 1)
            with ve.Fori(0, NL // B) as i:
                for u in range(B):
                    n = i * B + u
                    ve.wait_ge(rows_in[u], i * 96 + 96 + START)
                    ve.tensor_tensor(ys[:, :], y[u][:, 0, :], y[u][:, 1, :], ALU.add).then_inc(ys_ok, 1)
                    ve.wait_ge(ys_ok, n + 1 + START)
                    for h in range(WH):
                        ve.bn_stats(st6[:, h, :], heads(ys)[:, h, :]).then_inc(bn, 1)
                    ve.wait_ge(bn, (n + 1) * WH + START)
                    ve.sem_inc(stats, 1)
                    for h in range(WH):
                        ve.bn_aggr(mv[:, h, :], st6[:, h, :]).then_inc(aggr, 1)
                    ve.wait_ge(aggr, (n + 1) * WH + START)
                    ve.tensor_tensor(heads(yc), heads(ys), wide(mv[:, :, 0:1]), ALU.subtract).then_inc(yc_ok, 1)
                    ve.wait_ge(rooted, n + 1 + START)
                    ve.reciprocal(rs[:, :], sd[:, :]).then_inc(rec, 1)
                    ve.wait_ge(rec, n + 2 + START)
                    ve.wait_ge(yc_ok, n + 1 + START)
                    ve.wait_ge(y_turned, i * B + START)
                    ve.tensor_tensor(heads(yn[u]), heads(yc), wide(rs[:, :, None]), ALU.mult).then_inc(yn_ok, 1)
                    ve.wait_ge(b_turned, n + 1 + START)
                    ve.wait_ge(wg_ok, n + START)
                    ve.tensor_tensor(wb[:, :, :], bp[u][:, :, :], v[u][:, :, :], ALU.mult).then_inc(wb_ok, 1)

        @block.scalar
        def _(act):
            act.wait_ge(const_in, 48 + START)
            with act.Fori(0, NL // B) as i:
                for u in range(B):
                    n = i * B + u
                    act.wait_ge(aggr, (n + 1) * WH + START)
                    act.wait_ge(rec, n + 1 + START)
                    act.activation(sd[:, :], mv[:, :, 1], ACT.Sqrt, bias=eps[:, :]).then_inc(rooted, 1)
                    act.wait_ge(y_turned, n + 1 + START)
                    act.wait_ge(wg_ok, n + START)
                    for q in range(4):
                        ins = act.activation(wn[:, q, :], yp[u][:, q, :], ACT.Identity, scale=ln[:, 0, q:q + 1], bias=ln[:, 1, q:q + 1])
                    ins.then_inc(wn_ok, 1)

        @block.tensor
        def _(pe):
            pe.wait_ge(const_in, 48 + START)
            with pe.Fori(0, NL // B) as i:
                for u in range(B):
                    n = i * B + u
                    pe.wait_ge(be_ok, n + 1 + START)
                    pe.wait_ge(wb_ok, i * B + START)
                    for q in range(4):
                        t = pe.transpose(bp[u][:, q, :], be[u][:, q * P:(q + 1) * P], ident[:, :])
                    t.then_inc(b_turned, 1)
                    pe.wait_ge(yn_ok, n + 1 + START)
                    pe.wait_ge(wn_ok, i * B + START)
                    for q in range(4):
                        t = pe.transpose(yp[u][:, q, :], yn[u][:, q * P:(q + 1) * P], ident[:, :])
                    t.then_inc(y_turned, 1)


def branch_products(nc, T):
    W, NB, NM = 512, LAT // 512, KT
    with Room(nc, "brp") as room:
        sb, sem = room.sb, room.sem
        stage = [sb(f"stage{u}", [P, D]) for u in range(2)]
        wh, wl = sb("wh", [P, 2, 4, D], F32R), sb("wl", [P, 2, 4, D], F32R)
        raw = [sb(f"raw{b}", [P, 4, W]) for b in range(2)]
        yh, yl = [[[sb(f"{n}{u}{b}", [P, 4, W], F32R) for b in range(2)] for u in range(2)] for n in ("yh", "yl")]
        gate = [sb(f"gate{u}", [P, 2, 4, W]) for u in range(2)]
        t = [[sb(f"t{u}{b}", [P, W]) for b in range(2)] for u in range(2)]
        mix = [sb(f"mix{u}", [P, W]) for u in range(2)]
        acc = [room.ps(f"acc{j}", [P, W]) for j in range(8)]
        w_in, raw_in, gate_in, m_out = [[sem(f"{n}{u}") for u in range(2)] for n in ("w_in", "raw_in", "gate_in", "m_out")]
        spent, w_hi, w_lo, y_hi, y_lo, made, gated, mixed = [sem(n) for n in ("spent", "w_hi", "w_lo", "y_hi", "y_lo", "made", "gated", "mixed")]
        wsrc = [T["w_br_ret"][0].rearrange("(k p) d -> k p d", p=P), T["w_br_rwkv"][0].rearrange("(k p) d -> k p d", p=P)]
        ysrc = [T[n].rearrange("(k p) t -> p k t", p=P) for n in ("yrT", "ywT")]
        gsrc = [T["zT"][(Z_MG + 8 * b) * P:(Z_MG + 8 * b + 8) * P, :].rearrange("(m p) t -> p m t", p=P) for b in range(2)]
        mT = T["mixT"].rearrange("(m p) t -> m p t", p=P)
        block = room.block()

        def blocks(eng, body):
            with eng.Fori(0, NB // 2) as i:
                for u in range(2):
                    body(u, i * 2 + u, i)

        @block.sync
        def _(sp):
            for j in range(8):
                if j >= 2:
                    sp.wait_ge(w_lo, j - 1 + START)
                sp.dma_start(stage[j % 2][:, :], wsrc[j // 4][j % 4]).then_inc(w_in[j % 2], 16)
            for b in range(2):
                sp.dma_start(raw[b][:, :, :], ysrc[b][:, :, 0:W]).then_inc(raw_in[b], 16)

            def load(h, at):
                for b in range(2):
                    sp.dma_start(gate[h][:, b, :, :], gsrc[b][:, 4 * h:4 * h + 4, ds(at, W)]).then_inc(gate_in[h], 16)
            for h in range(2):
                load(h, CTX)

            def body(u, n, i):
                here, at, gate_at = sp.snap(n * W), sp.snap(((n + 1) % NB) * W), sp.snap(((n + 1) % NB) * W + CTX)
                for b in range(2):
                    sp.wait_ge(y_lo, n * 2 + (b + 1) + START)
                    sp.sem_inc(spent, 1)
                    sp.dma_start(raw[b][:, :, :], ysrc[b][:, :, ds(at, W)]).then_inc(raw_in[b], 16)
                for m in range(NM):
                    sp.wait_ge(mixed, n * NM + (m + 1) + START)
                    sp.sem_inc(spent, 1)
                    sp.dma_start(mT[m, :, ds(here, W)], mix[m % 2][:, :]).then_inc(m_out[m % 2], 16)
                    if m % 4 == 3:
                        load(m // 4, gate_at)
            blocks(sp, body)
            for s in range(2):
                sp.wait_ge(m_out[s], 8 * NM * NB + START)
                sp.wait_ge(gate_in[s], 32 * (NB + 1) + START)
                sp.wait_ge(raw_in[s], 16 * (NB + 1) + START)

        @block.gpsimd
        def _(gp):

            def body(u, n, i):
                for m in range(NM):
                    s = m % 2
                    gp.wait_ge(gated, n * (2 * NM) + (2 * m + 2) + START)
                    gp.wait_ge(m_out[s], n * (8 * NM) + 16 * (m // 2) + START)
                    gp.tensor_tensor(mix[s][:, :], t[s][0][:, :], t[s][1][:, :], ALU.add).then_inc(mixed, 1)
            blocks(gp, body)

        @block.scalar
        def _(act):
            for j in range(8):
                act.wait_ge(w_in[j % 2], 16 * (j // 2 + 1) + START)
                act.activation(wh[:, j // 4, j % 4, :], stage[j % 2][:, :], ACT.Copy).then_inc(w_hi, 1)

            def body(u, n, again):
                for b in range(2):
                    act.wait_ge(raw_in[b], n * 16 + 16 + START)
                    if again:
                        act.wait_ge(made, (n - 1) * (2 * NM) + START)
                    act.activation(yh[u][b][:, :, :], raw[b][:, :, :], ACT.Copy).then_inc(y_hi, 1)
            for u in range(2):
                body(u, u, False)
            with act.Fori(1, NB // 2) as i:
                for u in range(2):
                    body(u, i * 2 + u, True)

        @block.vector
        def _(ve):
            for j in range(8):
                ve.wait_ge(w_hi, j + 1 + START)
                ve.tensor_tensor(wl[:, j // 4, j % 4, :], stage[j % 2][:, :], wh[:, j // 4, j % 4, :], ALU.subtract).then_inc(w_lo, 1)

            def split(u, n):
                for b in range(2):
                    ve.wait_ge(y_hi, n * 2 + (b + 1) + START)
                    ve.tensor_tensor(yl[u][b][:, :, :], raw[b][:, :, :], yh[u][b][:, :, :], ALU.subtract).then_inc(y_lo, 1)

            def gates(n, i):
                for m in range(NM):
                    s = m % 2
                    if m % 4 == 0:
                        ve.wait_ge(gate_in[m // 4], n * 32 + 32 + START)
                    if m >= 2:
                        ve.wait_ge(mixed, n * NM + (m - 1) + START)
                    else:
                        ve.wait_ge(mixed, n * NM + START)
                    for b in range(2):
                        ve.wait_ge(made, n * (2 * NM) + (2 * m + b + 1) + START)
                        ve.tensor_tensor(t[s][b][:, :], acc[(2 * m + b) % 8][:, :], gate[m // 4][:, b, m % 4, :], ALU.mult).then_inc(gated, 1)
            split(0, 0)
            with ve.Fori(0, NB // 2 - 1) as i:
                split(1, i * 2 + 1)
                gates(i * 2, i)
                split(0, i * 2 + 2)
                gates(i * 2 + 1, i)
            split(1, NB - 1)
            gates(NB - 2, 0)
            gates(NB - 1, 0)

        @block.tensor
        def _(pe):
            pe.wait_ge(w_lo, 8 + START)

            def body(u, n, i):
                for m in range(NM):
                    for b in range(2):
                        if m == 0:
                            pe.wait_ge(y_lo, n * 2 + (b + 1) + START)
                        g = 2 * m + b
                        if g < 8:
                            pe.wait_ge(gated, n * (2 * NM) + START)
                        else:
                            pe.wait_ge(gated, n * (2 * NM) + (g - 7) + START)
                        for k in range(4):
                            c = slice(m * P, (m + 1) * P)
                            mm = product(pe, acc[g % 8][:, :], (wh[:, b, k, c], wl[:, b, k, c]),
                                         (yh[u][b][:, k, :], yl[u][b][:, k, :]), k == 0, k == 3)
                        mm.then_inc(made, 1)
            blocks(pe, body)


def mixer_output(nc, T):
    NL = LAT // P
    with Room(nc, "mxo") as room:
        sb, sem = room.sb, room.sem
        stage = [sb(f"stage{u}", [P, D]) for u in range(2)]
        wh, wl = sb("wh", [P, KT, D], F32R), sb("wl", [P, KT, D], F32R)
        mh, ml = [[sb(f"{n}{u}", [P, KT, P], F32R) for u in range(2)] for n in ("mh", "ml")]
        m, x, yg, x1, xh = [[sb(f"{n}{u}", [P, KT, P] if n == "m" else [P, D]) for u in range(2)] for n in ("m", "x", "yg", "x1", "xh")]
        sq, g1, ng, gg, eps = sb("sq", [P, D]), sb("g1", [P, D]), sb("ng", [P, D]), sb("gg", [P, D]), sb("eps", [P, 1])
        ss, rt, rs = [[[sb(f"{n}{j}{u}", [P, 1]) for u in range(2)] for j in range(2)] for n in ("ss", "rt", "rs")]
        acc = [room.ps(f"acc{u}", [P, D]) for u in range(2)]
        w_in, m_in, x_in, x1_out, xh_out = [[sem(f"{n}{u}") for u in range(2)] for n in ("w_in", "m_in", "x_in", "x1_out", "xh_out")]
        (const_in, gg_ok, w_hi, w_lo, m_hi, m_lo, made, sums, rooted, rec, sums2, rooted2, rec2, yg_ok, x1_ok, xh_ok, spent) = [sem(n) for n in (
            "const_in", "gg_ok", "w_hi", "w_lo", "m_hi", "m_lo", "made", "sums", "rooted", "rec", "sums2", "rooted2", "rec2", "yg_ok",
            "x1_ok", "xh_ok", "spent")]
        wsrc = T["w_out"][0].rearrange("(k p) d -> k p d", p=P)
        msrc = T["mixT"].rearrange("(k p) t -> p k t", p=P)
        xsrc = T["tokens"]
        block = room.block()

        @block.sync
        def _(sp):
            sp.dma_start(g1[:, :], T["mod_rows"][0:1, 2 * D:3 * D].to_broadcast([P, D])).then_inc(const_in, 16)
            sp.dma_start(ng[:, :], T["norm_g"][0, 1:2, :].to_broadcast([P, D])).then_inc(const_in, 16)
            for u in range(2):
                sp.dma_start(m[u][:, :, :], msrc[:, :, u * P:(u + 1) * P]).then_inc(m_in[u], 16)
                sp.dma_start(x[u][:, :], xsrc[CTX + u * P:CTX + (u + 1) * P, :]).then_inc(x_in[u], 16)
            for k in range(KT):
                if k >= 2:
                    sp.wait_ge(w_lo, k - 1 + START)
                sp.dma_start(stage[k % 2][:, :], wsrc[k]).then_inc(w_in[k % 2], 16)
            with sp.Fori(0, NL // 2 - 1) as i:
                for u in range(2):
                    at, row = sp.snap(i * (2 * P) + (2 + u) * P), sp.snap(i * (2 * P) + (CTX + (2 + u) * P))
                    count = sp.snap(i * 2 + (u + 1) + START)
                    here = sp.snap(i * (2 * P) + u * P)
                    sp.wait_ge(m_lo, count)
                    sp.sem_inc(spent, 1)
                    sp.dma_start(m[u][:, :, :], msrc[:, :, ds(at, P)]).then_inc(m_in[u], 16)
                    sp.wait_ge(x1_ok, count)
                    sp.sem_inc(spent, 1)
                    sp.dma_start(x[u][:, :], xsrc[ds(row, P), :]).then_inc(x_in[u], 16)
                    sp.dma_start(T["x1"][ds(here, P), :], x1[u][:, :]).then_inc(x1_out[u], 16)
                    sp.wait_ge(xh_ok, count)
                    sp.sem_inc(spent, 1)
                    sp.dma_start(T["xh"][ds(here, P), :], xh[u][:, :]).then_inc(xh_out[u], 16)
            for u in range(2):
                rows = slice(LAT + (u - 2) * P, LAT + (u - 1) * P)
                sp.wait_ge(x1_ok, NL - 1 + u + START)
                sp.dma_start(T["x1"][rows, :], x1[u][:, :]).then_inc(x1_out[u], 16)
                sp.wait_ge(xh_ok, NL - 1 + u + START)
                sp.dma_start(T["xh"][rows, :], xh[u][:, :]).then_inc(xh_out[u], 16)
            for u in range(2):
                sp.wait_ge(x1_out[u], 8 * NL + START)
                sp.wait_ge(xh_out[u], 8 * NL + START)

        def pairs(eng, body):
            with eng.Fori(0, NL // 2) as i:
                for u in range(2):
                    body(u, i, i * 2 + u)

        @block.scalar
        def _(act):
            for u in range(2):
                act.wait_ge(m_in[u], 16 + START)
                act.activation(mh[u][:, :, :], m[u][:, :, :], ACT.Copy).then_inc(m_hi, 1)
            for k in range(KT):
                act.wait_ge(w_in[k % 2], 16 * (k // 2 + 1) + START)
                act.activation(wh[:, k, :], stage[k % 2][:, :], ACT.Copy).then_inc(w_hi, 1)
            act.wait_ge(gg_ok, 1 + START)

            def body(u, i, n):
                act.wait_ge(made, n + 1 + START)
                act.wait_ge(rec, n + START)
                act.activation(sq[:, :], acc[u][:, :], ACT.Square, accum_out=ss[0][u][:, :]).then_inc(sums, 1)
                act.wait_ge(sums, n + 1 + START)
                act.activation(rt[0][u][:, :], ss[0][u][:, :], ACT.Sqrt, scale=1.0 / D, bias=eps[:, :]).then_inc(rooted, 1)
                act.wait_ge(x1_ok, n + 1 + START)
                act.activation(sq[:, :], x1[u][:, :], ACT.Square, accum_out=ss[1][u][:, :]).then_inc(sums2, 1)
                act.wait_ge(sums2, n + 1 + START)
                act.activation(rt[1][u][:, :], ss[1][u][:, :], ACT.Sqrt, scale=1.0 / D, bias=eps[:, :]).then_inc(rooted2, 1)
                if isinstance(i, int):
                    return
                act.wait_ge(m_in[u], i * 16 + 32 + START)
                act.activation(mh[u][:, :, :], m[u][:, :, :], ACT.Copy).then_inc(m_hi, 1)
            with act.Fori(0, NL // 2 - 1) as i:
                for u in range(2):
                    body(u, i, i * 2 + u)
            for u in range(2):
                body(u, NL // 2 - 1, NL - 2 + u)

        @block.vector
        def _(ve):
            ve.memset(eps[:, :], EPS)
            ve.wait_ge(const_in, 32 + START)
            ve.tensor_tensor(gg[:, :], g1[:, :], ng[:, :], ALU.mult).then_inc(gg_ok, 1)
            for u in range(2):
                ve.wait_ge(m_hi, u + 1 + START)
                ve.tensor_tensor(ml[u][:, :, :], m[u][:, :, :], mh[u][:, :, :], ALU.subtract).then_inc(m_lo, 1)
            for k in range(KT):
                ve.wait_ge(w_hi, k + 1 + START)
                ve.tensor_tensor(wl[:, k, :], stage[k % 2][:, :], wh[:, k, :], ALU.subtract).then_inc(w_lo, 1)
            ve.wait_ge(gg_ok, 1 + START)

            def body(u, i, n):
                ve.wait_ge(rooted, n + 1 + START)
                ve.reciprocal(rs[0][u][:, :], rt[0][u][:, :]).then_inc(rec, 1)
                ve.wait_ge(rec, n + 1 + START)
                ve.scalar_tensor_tensor(yg[u][:, :], acc[u][:, :], rs[0][u][:, 0:1], gg[:, :], ALU.mult, ALU.mult).then_inc(yg_ok, 1)
                ve.wait_ge(yg_ok, n + 1 + START)
                ve.wait_ge(x_in[u], (n + (2 - u)) * 8 + START)
                if isinstance(i, int):
                    ve.wait_ge(x1_out[u], 16 * i + START)
                else:
                    ve.wait_ge(x1_out[u], i * 16 + START)
                ve.tensor_tensor(x1[u][:, :], yg[u][:, :], x[u][:, :], ALU.add).then_inc(x1_ok, 1)
                ve.wait_ge(rooted2, n + 1 + START)
                ve.reciprocal(rs[1][u][:, :], rt[1][u][:, :]).then_inc(rec2, 1)
                ve.wait_ge(rec2, n + 1 + START)
                ve.wait_ge(xh_out[u], i * 16 + START)
                ve.tensor_scalar(xh[u][:, :], x1[u][:, :], rs[1][u][:, 0:1], None, ALU.mult).then_inc(xh_ok, 1)
                if isinstance(i, int):
                    return
                ve.wait_ge(m_hi, n + 3 + START)
                ve.tensor_tensor(ml[u][:, :, :], m[u][:, :, :], mh[u][:, :, :], ALU.subtract).then_inc(m_lo, 1)
            with ve.Fori(0, NL // 2 - 1) as i:
                for u in range(2):
                    body(u, i, i * 2 + u)
            for u in range(2):
                body(u, NL // 2 - 1, NL - 2 + u)

        @block.tensor
        def _(pe):
            pe.wait_ge(w_lo, KT + START)

            def body(u, i, n):
                pe.wait_ge(m_lo, n + 1 + START)
                pe.wait_ge(yg_ok, i * 2 + START)
                for half in range(2):
                    c = slice(half * 512, half * 512 + 512)
                    for k in range(KT):
                        mm = product(pe, acc[u][:, c], (mh[u][:, k, :], ml[u][:, k, :]), (wh[:, k, c], wl[:, k, c]), k == 0, k == KT - 1)
                mm.then_inc(made, 1)
            pairs(pe, body)


def router(nc, T):
    NL = LAT // P
    with Room(nc, "rou") as room:
        sb, sem = room.sb, room.sem
        ident, wr = sb("ident", [P, P]), sb("wr", [P, KT, NE])
        mod, gain, scale, scale1 = sb("mod", [P, 2, KT]), sb("gain", [P, KT]), sb("scale", [P, KT]), sb("scale1", [P, KT])
        x, h, ex, af = [[sb(f"{n}{u}", s) for u in range(2)] for n, s in (
            ("x", [P, D]), ("h", [P, KT, P]), ("ex", [P, NE]), ("af", [P, NE]))]
        mx, den, rden = sb("mx", [P, 1]), sb("den", [P, 1]), sb("rden", [P, 1])
        affT = sb("affT", [NE, LAT])
        tp = [room.ps(f"tp{u}", [P, KT, P]) for u in range(2)]
        lg, ap = [[room.ps(f"{n}{u}", s) for u in range(2)] for n, s in (("lg", [P, NE]), ("ap", [NE, P]))]
        x_in = [sem(f"x_in{u}") for u in range(2)]
        (const_in, setup, spent, turned, h_ok, h_rest, made, mx_ok, ex_ok, den_ok, af_ok, a_turned, a_ok, out) = [sem(n) for n in (
            "const_in", "setup", "spent", "turned", "h_ok", "h_rest", "made", "mx_ok", "ex_ok", "den_ok", "af_ok", "a_turned", "a_ok", "out")]
        block = room.block()

        @block.sync
        def _(sp):
            sp.dma_start(ident[:, :], T["ident"]).then_inc(const_in, 16)
            sp.dma_start(wr[:, :, :], T["w_router"][0].rearrange("(k p) e -> p k e", p=P)).then_inc(const_in, 16)
            with nc.allow_non_contiguous_dma("channel parameters over partitions"):
                for j in range(2):
                    sp.dma_start(mod[:, j, :], T["mod_rows"][0:1, (3 + j) * D:(4 + j) * D]
                                 .rearrange("a (t p) -> p (a t)", p=P)).then_inc(const_in, 16)
                sp.dma_start(gain[:, :], T["norm_g"][0, 2:3, :].rearrange("a (t p) -> p (a t)", p=P)).then_inc(const_in, 16)
            for u in range(2):
                sp.dma_start(x[u][:, :], T["xh"][u * P:(u + 1) * P, :]).then_inc(x_in[u], 16)
            with sp.Fori(0, NL // 2 - 1) as i:
                for u in range(2):
                    at = sp.snap(i * (2 * P) + (2 + u) * P)
                    sp.wait_ge(turned, sp.snap(i * 2 + (u + 1) + START))
                    sp.sem_inc(spent, 1)
                    sp.dma_start(x[u][:, :], T["xh"][ds(at, P), :]).then_inc(x_in[u], 16)
            sp.wait_ge(a_ok, NL + START)
            sp.dma_start(T["affT"], affT[:, :]).then_inc(out, 16)
            sp.wait_ge(out, 16 + START)

        def ahead(eng, move, soft):
            move(0, 0)
            with eng.Fori(0, NL // 2 - 1) as i:
                for u in range(2):
                    move(1 - u, i * 2 + (u + 1))
                    soft(u, i * 2 + u)
            move(1, NL - 1)
            soft(0, NL - 2)
            soft(1, NL - 1)

        @block.tensor
        def _(pe):
            pe.wait_ge(const_in, 16 * 5 + START)

            def turn(u, n):
                pe.wait_ge(x_in[u], (n - u) * 8 + 16 + START)
                if not isinstance(n, int):
                    for moved in (h_ok, h_rest):
                        pe.wait_ge(moved, n - 1 + START)
                for k in range(KT):
                    t = pe.transpose(tp[u][:, k, :], x[u][:, k * P:(k + 1) * P], ident[:, :])
                t.then_inc(turned, 1)
            for u in range(2):
                turn(u, u)

            def logits(u, i, n):
                pe.wait_ge(h_ok, n + 1 + START)
                pe.wait_ge(h_rest, n + 1 + START)
                pe.wait_ge(ex_ok, i * 2 + START)
                for k in range(KT):
                    mm = pe.matmul(lg[u][:, :], h[u][:, k, :], wr[:, k, :], start=(k == 0), stop=(k == KT - 1))
                mm.then_inc(made, 1)

            def back(u, i, n):
                pe.wait_ge(af_ok, n + 1 + START)
                pe.wait_ge(a_ok, i * 2 + START)
                pe.transpose(ap[u][:, :], af[u][:, :], ident[:, :]).then_inc(a_turned, 1)

            with pe.Fori(0, NL // 2 - 1) as i:
                for u in range(2):
                    logits(u, i, i * 2 + u)
                    turn(u, i * 2 + (2 + u))
                    back(u, i, i * 2 + u)
            for u in range(2):
                n = NL - 2 + u
                logits(u, NL // 2 - 1, n)
                back(u, NL // 2 - 1, n)

        @block.scalar
        def _(act):
            act.wait_ge(setup, 2 + START)

            def move(u, n):
                act.wait_ge(turned, n + 1 + START)
                act.wait_ge(made, max(n - 1, 0) + START if isinstance(n, int) else n - 1 + START)
                for k in range(KT // 2):
                    ins = act.activation(h[u][:, k, :], tp[u][:, k, :], ACT.Identity, scale=scale[:, k:k + 1], bias=mod[:, 0, k:k + 1])
                ins.then_inc(h_ok, 1)

            def soft(u, n):
                act.wait_ge(mx_ok, n + 1 + START)
                act.wait_ge(af_ok, n + START)
                act.activation(ex[u][:, :], lg[u][:, :], ACT.Exp, bias=mx[:, :], accum_out=den[:, :]).then_inc(ex_ok, 1)
                act.wait_ge(a_turned, n + 1 + START)
                act.activation(affT[:, ds(n * P, P)], ap[u][:, :], ACT.Copy).then_inc(a_ok, 1)
            ahead(act, move, soft)

        @block.vector
        def _(ve):
            ve.wait_ge(const_in, 16 * 5 + START)
            ve.tensor_scalar(scale1[:, :], mod[:, 1, :], 1.0, None, ALU.add).then_inc(setup, 1)
            ve.wait_ge(setup, 1 + START)
            ve.tensor_tensor(scale[:, :], scale1[:, :], gain[:, :], ALU.mult).then_inc(setup, 1)
            ve.wait_ge(setup, 2 + START)

            def move(u, n):
                ve.wait_ge(turned, n + 1 + START)
                ve.wait_ge(made, max(n - 1, 0) + START if isinstance(n, int) else n - 1 + START)
                for k in range(KT // 2, KT):
                    ins = ve.tensor_scalar(h[u][:, k, :], tp[u][:, k, :], scale[:, k:k + 1], mod[:, 0, k:k + 1], ALU.mult, ALU.add)
                ins.then_inc(h_rest, 1)

            def soft(u, n):
                ve.wait_ge(made, n + 1 + START)
                ve.wait_ge(ex_ok, n + START)
                ve.tensor_reduce(mx[:, :], lg[u][:, :], AX.X, ALU.max, negate=True).then_inc(mx_ok, 1)
                ve.wait_ge(ex_ok, n + 1 + START)
                ve.reciprocal(rden[:, :], den[:, :]).then_inc(den_ok, 1)
                ve.wait_ge(den_ok, n + 1 + START)
                ve.wait_ge(a_turned, max(n - 1, 0) + START if isinstance(n, int) else n - u + START)
                ve.tensor_scalar(af[u][:, :], ex[u][:, :], rden[:, 0:1], None, ALU.mult).then_inc(af_ok, 1)
            ahead(ve, move, soft)


def choose(nc, T):
    SEG = LAT // 8
    NBITS = 30
    CH = LAT // P
    with Room(nc, "cho") as room:
        sb, sem = room.sb, room.sem
        A = sb("A", [P, SEG])
        bits = sb("bits", [P, NBITS], I32)
        ident, same, before = sb("ident", [P, P]), sb("same", [P, P]), sb("before", [P, P])
        iota, ids = sb("iota", [P, CAP]), sb("ids", [P, 2, P, 2])
        iota16 = sb("iota16", [P, CAP], BF16)
        ge = sb("ge", [P, SEG])
        t, cand = sb("t", [P, 1], I32), sb("cand", [P, 1], I32)
        cnt, kept = sb("cnt", [P, 1]), sb("kept", [P, 1])
        gt, eq, pre, ok, pick, sel, run, posm = [sb(n, [P, SEG]) for n in ("gt", "eq", "pre", "ok", "pick", "sel", "run", "posm")]
        ones = sb("ones", [P, SEG])
        cg, ce, cs, need, thr, base = [sb(n, [P, 1]) for n in ("cg", "ce", "cs", "need", "thr", "base")]
        posT, affT = sb("posT", [P, 2, P]), sb("affT", [P, 2, P])
        rest = [sb(f"rest{j}", [P, 2, P]) for j in range(2)]
        info = sb("info", [P, 2, P, 5], BF16)
        hot = [sb(f"hot{u}", [P, CH, CAP], BF16) for u in range(2)]
        slots, gates = sb("slots", [P, NE, 2], I32), sb("gates", [P, NE, 2])
        tot = room.ps("tot", [P, 4])
        tp = room.ps("tp", [P, 2, 2, P])
        res = [room.ps(f"res{u}", [P, 2, 8]) for u in range(2)]
        const_in, out = sem("const_in"), sem("out")
        (cand_ok, ge_ok, cnt_ok, tot_ok, kept_ok, t_ok, step, summed, turned, moved, hot_ok, found, read, info_ok) = [sem(n) for n in (
            "cand_ok", "ge_ok", "cnt_ok", "tot_ok", "kept_ok", "t_ok", "step", "summed", "turned", "moved", "hot_ok", "found",
            "read", "info_ok")]
        f32 = lambda a: a[:, :].bitcast(F32)
        listed = sem("listed")
        parts, two = sb("parts", [P, NE, 2, 5]), sb("two", [P, NE, 2])
        block = room.block()

        @block.sync
        def _(sp):
            for dst, name in ((ident, "ident"), (same, "same_expert"), (before, "segments_before"), (iota, "iota"), (bits, "bits")):
                sp.dma_start(dst[:, :], T[name]).then_inc(const_in, 16)
            sp.dma_start(ids[:, :, :, :], T["token_ids"]).then_inc(const_in, 16)
            sp.dma_start(A[:, :], T["affT"].rearrange("e (s c) -> (e s) c", s=8)).then_inc(const_in, 16)
            sp.wait_ge(listed, 1 + START)
            sp.dma_start(T["slots"], slots[:, :, :]).then_inc(out, 16)
            sp.dma_start(T["gates"], gates[:, :, :]).then_inc(out, 16)
            sp.wait_ge(out, 32 + START)

        @block.vector
        def _(ve):
            st = Steps(ve, step)
            ve.wait_ge(const_in, 16 * 7 + START)
            ve.memset(t[:, :], 0)
            st.done(ve.memset(ones[:, :], 1.0))
            st.wait()
            with ve.Fori(0, NBITS) as i:
                ve.wait_ge(t_ok, i + START)
                ve.tensor_tensor(cand[:, :], t[:, :], bits[:, ds(i, 1)], ALU.bitwise_or).then_inc(cand_ok, 1)
                ve.wait_ge(cand_ok, i + 1 + START)
                ve.tensor_scalar(ge[:, :], A[:, :], f32(cand), None, ALU.is_ge).then_inc(ge_ok, 1)
                ve.wait_ge(ge_ok, i + 1 + START)
                ve.wait_ge(tot_ok, i + START)
                ve.tensor_reduce(cnt[:, :], ge[:, :], AX.X, ALU.add).then_inc(cnt_ok, 1)
                ve.wait_ge(tot_ok, i + 1 + START)
                ve.scalar_tensor_tensor(kept[:, :], tot[:, 0:1], float(CAP), f32(cand), ALU.is_ge, ALU.mult).then_inc(kept_ok, 1)
                ve.wait_ge(kept_ok, i + 1 + START)
                ve.tensor_tensor(f32(t), f32(t), kept[:, :], ALU.max).then_inc(t_ok, 1)
            ve.wait_ge(t_ok, NBITS + START)
            st.done(ve.tensor_scalar(gt[:, :], A[:, :], f32(t), None, ALU.is_gt))
            st.done(ve.tensor_scalar(eq[:, :], A[:, :], f32(t), None, ALU.is_equal))
            st.wait()
            ve.tensor_reduce(cg[:, :], gt[:, :], AX.X, ALU.add).then_inc(summed, 1)
            ve.tensor_reduce(ce[:, :], eq[:, :], AX.X, ALU.add).then_inc(summed, 1)
            st.done(ve.tensor_tensor_scan(pre[:, :], ones[:, :], eq[:, :], 0.0, ALU.mult, ALU.add))
            ve.wait_ge(tot_ok, NBITS + 1 + START)
            st.done(ve.tensor_scalar(need[:, :], tot[:, 1:2], -1.0, float(CAP), ALU.mult, ALU.add))
            st.wait()
            st.done(ve.tensor_tensor(thr[:, :], need[:, :], tot[:, 2:3], ALU.subtract))
            st.wait()
            st.done(ve.tensor_scalar(ok[:, :], pre[:, :], thr[:, 0:1], None, ALU.is_le))
            st.wait()
            st.done(ve.tensor_tensor(pick[:, :], ok[:, :], eq[:, :], ALU.mult))
            st.wait()
            st.done(ve.tensor_tensor(sel[:, :], pick[:, :], gt[:, :], ALU.add))
            st.wait()
            ve.tensor_reduce(cs[:, :], sel[:, :], AX.X, ALU.add).then_inc(summed, 1)
            st.done(ve.tensor_tensor_scan(run[:, :], ones[:, :], sel[:, :], 0.0, ALU.mult, ALU.add))
            ve.wait_ge(tot_ok, NBITS + 2 + START)
            st.done(ve.tensor_copy(base[:, :], tot[:, 3:4]))
            st.wait()
            st.done(ve.scalar_tensor_tensor(ok[:, :], run[:, :], base[:, 0:1], sel[:, :], ALU.add, ALU.mult))
            st.wait()
            ve.tensor_scalar(posm[:, :], ok[:, :], 1.0, None, ALU.subtract).then_inc(summed, 1)
            ve.wait_ge(turned, 1 + START)
            ve.tensor_copy(posT[:, :, :], tp[:, 0, :, :]).then_inc(moved, 1)
            ve.tensor_copy(affT[:, :, :], tp[:, 1, :, :]).then_inc(moved, 1)
            st.done(ve.tensor_copy(iota16[:, :], iota[:, :]))
            ve.tensor_copy(info[:, :, :, 0:2], ids[:, :, :, :]).then_inc(info_ok, 1)
            ve.wait_ge(moved, 2 + START)
            for j, src in enumerate((affT, rest[0], rest[1])):
                st.done(ve.tensor_copy(info[:, :, :, 2 + j], src[:, :, :]))
                st.wait()
                if j < 2:
                    st.done(ve.tensor_tensor(rest[j][:, :, :], src[:, :, :], info[:, :, :, 2 + j], ALU.subtract))
                    st.wait()
            ve.sem_inc(info_ok, 1)

            def mark(u, i, n):
                ve.wait_ge(found, i * 2 + START)
                for c in range(CH):
                    ins = ve.tensor_scalar(hot[u][:, c, :], iota16[:, :], posT[:, c % 2, ds(n * 8 + c // 2, 1)], None, ALU.is_equal)
                ins.then_inc(hot_ok, 1)

            with ve.Fori(0, NE // 2) as i:
                for u in range(2):
                    n = i * 2 + u
                    mark(u, i, n)
                    ve.wait_ge(found, n + 1 + START)
                    ve.tensor_copy(parts[:, ds(n, 1), :, :], res[u][:, None, :, 0:5]).then_inc(read, 1)
            ve.wait_ge(read, NE + START)
            st.done(ve.scalar_tensor_tensor(slots[:, :, :], parts[:, :, :, 0], float(P), parts[:, :, :, 1], ALU.mult, ALU.add))
            st.done(ve.tensor_tensor(two[:, :, :], parts[:, :, :, 2], parts[:, :, :, 3], ALU.add))
            st.wait()
            st.done(ve.tensor_tensor(gates[:, :, :], two[:, :, :], parts[:, :, :, 4], ALU.add))
            st.wait()
            ve.sem_inc(listed, 1)

        @block.tensor
        def _(pe):
            pe.wait_ge(const_in, 16 * 7 + START)
            with pe.Fori(0, NBITS) as i:
                pe.wait_ge(cnt_ok, i + 1 + START)
                pe.wait_ge(kept_ok, i + START)
                pe.matmul(tot[:, 0:1], same[:, :], cnt[:, :], start=True, stop=True).then_inc(tot_ok, 1)
            pe.wait_ge(summed, 2 + START)
            pe.matmul(tot[:, 1:2], same[:, :], cg[:, :], start=True, stop=True)
            pe.matmul(tot[:, 2:3], before[:, :], ce[:, :], start=True, stop=True).then_inc(tot_ok, 1)
            pe.wait_ge(summed, 3 + START)
            pe.matmul(tot[:, 3:4], before[:, :], cs[:, :], start=True, stop=True).then_inc(tot_ok, 1)
            pe.wait_ge(summed, 4 + START)
            for h in range(2):
                pe.transpose(tp[:, 0, h, :], posm[:, h * P:(h + 1) * P], ident[:, :])
                m = pe.transpose(tp[:, 1, h, :], A[:, h * P:(h + 1) * P], ident[:, :])
            m.then_inc(turned, 1)
            pe.wait_ge(info_ok, 2 + START)
            with pe.Fori(0, NE // 2) as i:
                for u in range(2):
                    n = i * 2 + u
                    pe.wait_ge(hot_ok, n + 1 + START)
                    pe.wait_ge(read, i * 2 + START)
                    for h in range(2):
                        for c in range(CH):
                            m = pe.matmul(res[u][:, h, 0:5], hot[u][:, c, h * P:(h + 1) * P], info[:, c % 2, ds(n * 8 + c // 2, 1), :],
                                          start=(c == 0), stop=(c == CH - 1))
                    m.then_inc(found, 1)


def experts(nc, T):
    NC, W = 6, 512
    ALL = NE * NC
    ZEROED = 8 * (LAT // P)
    with Room(nc, "exp") as room:
        sb, sem = room.sb, room.sem
        ident, zero = sb("ident", [P, P]), sb("zero", [P, D])
        mod, gain, scale, scale1 = sb("mod", [P, 2, KT]), sb("gain", [P, KT]), sb("scale", [P, KT]), sb("scale1", [P, KT])
        slots, gates = sb("slots", [P, NE, 2], I32), sb("gates", [P, NE, 2])
        raw = [sb(f"raw{s}", [P, KT, W]) for s in range(2)]
        wh, wl = [[sb(f"{n}{s}", [P, KT, W], F32R) for s in range(2)] for n in ("wh", "wl")]
        xg = [sb(f"xg{t}", [P, D]) for t in range(2)]
        hx, xh, xl = sb("hx", [P, KT, CAP]), sb("xh", [P, KT, CAP], F32R), sb("xl", [P, KT, CAP], F32R)
        sg, hv = sb("sg", [P, 4, CAP]), sb("hv", [P, 4, CAP])
        hh, hl = sb("hh", [P, 8, CAP], F32R), sb("hl", [P, 8, CAP], F32R)
        rows = [[sb(f"rows{u}{t}", [P, D]) for t in range(2)] for u in range(2)]
        offs = [[sb(f"offs{u}{t}", [P, 1], I32) for t in range(2)] for u in range(2)]
        gsc = [sb(f"gsc{u}", [P, 2]) for u in range(2)]
        acc = [room.ps(f"acc{a}", [P, 4, CAP]) for a in range(3)]
        tp = room.ps("tp", [P, KT, P])
        w_in = [sem(f"w_in{s}") for s in range(2)]
        x_in, added = [[sem(f"{n}{s}", start=0) for s in range(2)] for n in ("x_in", "added")]
        (const_in, setup, zero_ok, w_hi, w_lo, made, turned, hx_ok, x_hi, x_lo, silu_ok, hid_ok, h_hi, h_lo, rows_ok,
         lists_ok, spent, spent_v) = [sem(n) for n in ("const_in", "setup", "zero_ok", "w_hi", "w_lo", "made", "turned", "hx_ok",
                                              "x_hi", "x_lo", "silu_ok", "hid_ok", "h_hi", "h_lo", "rows_ok", "lists_ok", "spent", "spent_v")]
        wx = T["w_x"]
        moe = T["moe"]
        block = room.block()

        def experts_of(eng, body):
            with eng.Fori(0, NE // 2) as i:
                for u in range(2):
                    body(u, i, i * 2 + u)

        @block.sync
        def _(sp):
            sp.dma_start(ident[:, :], T["ident"]).then_inc(const_in, 16)
            sp.dma_start(slots[:, :, :], T["slots"]).then_inc(const_in, 16)
            sp.dma_start(gates[:, :, :], T["gates"]).then_inc(const_in, 16)
            with nc.allow_non_contiguous_dma("channel parameters over partitions"):
                for j in range(2):
                    sp.dma_start(mod[:, j, :], T["mod_rows"][0:1, (3 + j) * D:(4 + j) * D]
                                 .rearrange("a (t p) -> p (a t)", p=P)).then_inc(const_in, 16)
                sp.dma_start(gain[:, :], T["norm_g"][0, 2:3, :].rearrange("a (t p) -> p (a t)", p=P)).then_inc(const_in, 16)
            for s in range(2):
                sp.dma_start(raw[s][:, :, :], wx[s]).then_inc(w_in[s], 16)
            with sp.Fori(0, ALL // 2) as i:
                for s in range(2):
                    chunk = sp.snap((i * 2 + (2 + s)) % ALL)
                    sp.wait_ge(w_lo, sp.snap(i * 2 + (s + 1) + START))
                    sp.sem_inc(spent, 1)
                    sp.dma_start(raw[s][:, :, :], wx[ds(chunk, 1)]).then_inc(w_in[s], 16)
            for s in range(2):
                sp.wait_ge(w_in[s], 16 * (ALL // 2 + 1) + START)

        @block.gpsimd
        def _(gp):
            gp.memset(zero[:, :], 0.0).then_inc(zero_ok, 1)
            gp.wait_ge(zero_ok, 1 + START)
            def gather(u):
                for t in range(2):
                    gp.indirect_dma_start(xg[t][:, :], None, T["xh"], bass.IndirectOffsetOnAxis(offs[u][t][:, 0:1], 0)).then_inc(x_in[t], 16)
            gp.wait_ge(lists_ok, 4 + START)
            gather(0)
            for n in range(LAT // P):
                gp.dma_start(moe[n * P:(n + 1) * P, :], zero[:, :]).then_inc(added[n % 2], 16)
            for u in range(2):
                gp.wait_ge(added[u], ZEROED)

            def body(u, i, n):
                gp.wait_ge(turned, n * 2 + 2 + START)
                gp.sem_inc(spent, 1)
                gp.wait_ge(lists_ok, n * 4 + 8 + START)
                gp.sem_inc(spent, 1)
                gather(1 - u)
                gp.wait_ge(rows_ok, n * 2 + 3 + START)
                gp.sem_inc(spent, 1)
                gp.wait_ge(added[1 - u], i * 32 + 32 * u + ZEROED)
                gp.sem_inc(spent, 1)
                for t in range(2):
                    gp.indirect_dma_start(moe, bass.IndirectOffsetOnAxis(offs[u][t][:, 0:1], 0), rows[u][t][:, :], None,
                                          compute_op=ALU.add).then_inc(added[u], 16)
            experts_of(gp, body)
            for u in range(2):
                gp.wait_ge(added[u], 16 * NE + ZEROED)
            for t in range(2):
                gp.wait_ge(x_in[t], 16 * (NE + 1))

        @block.tensor
        def _(pe):
            def turn(t, n):
                pe.wait_ge(x_in[t], n * 16 + 16)
                pe.wait_ge(hx_ok, n * 2 + t + START)
                for k in range(KT):
                    m = pe.transpose(tp[:, k, :], xg[t][:, k * P:(k + 1) * P], ident[:, :])
                m.then_inc(turned, 1)
            pe.wait_ge(const_in, 16 * 6 + START)
            turn(0, 0)
            turn(1, 0)

            def body(u, i, n):
                pe.wait_ge(x_lo, n * 2 + 2 + START)
                free = [(hid_ok, n * 2), (rows_ok, n * 2), (rows_ok, n * 2 + 1), (silu_ok, n * 2 + 1), (hid_ok, n * 2 + 1), (silu_ok, n * 2 + 2)]
                for j in range(NC):
                    s, a = j % 2, acc[j % 3]
                    pe.wait_ge(w_lo, n * NC + (j + 1) + START)
                    pe.wait_ge(free[j][0], free[j][1] + START)
                    if j < 4:
                        for m in range(4):
                            c = slice(m * P, (m + 1) * P)
                            for k in range(KT):
                                mm = product(pe, a[:, m, :], (wh[s][:, k, c], wl[s][:, k, c]), (xh[:, k, :], xl[:, k, :]), k == 0, k == KT - 1)
                    else:
                        out = a[:, :, :].rearrange("p (t x) c -> p t (x c)", t=2)
                        for t in range(2):
                            c = slice(t * P, (t + 1) * P)
                            for k in range(8):
                                if j == 4 and t == 0 and k % 4 == 0:
                                    pe.wait_ge(h_lo, n * 2 + (k // 4 + 1) + START)
                                mm = product(pe, out[:, t, :], (hh[:, k, c], hl[:, k, c]), (wh[s][:, k, :], wl[s][:, k, :]), k == 0, k == 7)
                    mm.then_inc(made, 1)
                    if j in (3, 4):
                        turn(j - 3, n + 1)
            experts_of(pe, body)

        @block.scalar
        def _(act):
            def move(t, n):
                act.wait_ge(turned, n * 2 + (t + 1) + START)
                act.wait_ge(x_lo, n * 2 + START)
                for k in range(KT):
                    ins = act.activation(hx[:, k, t * P:(t + 1) * P], tp[:, k, :], ACT.Identity, scale=scale[:, k:k + 1], bias=mod[:, 0, k:k + 1])
                ins.then_inc(hx_ok, 1)
                act.wait_ge(hx_ok, n * 2 + (t + 1) + START)
                act.activation(xh[:, :, t * P:(t + 1) * P], hx[:, :, t * P:(t + 1) * P], ACT.Copy).then_inc(x_hi, 1)

            def split(s, c):
                act.wait_ge(w_in[s], (c - s) * 8 + 16 + START)
                act.activation(wh[s][:, :, :], raw[s][:, :, :], ACT.Copy).then_inc(w_hi, 1)
            split(0, 0)
            act.wait_ge(setup, 2 + START)
            act.sem_inc(rows_ok, 1)
            move(0, 0)
            move(1, 0)

            def body(u, i, n):
                for j in range(NC):
                    c = n * NC + j
                    act.wait_ge(made, c + START)
                    split(1 - j % 2, c + 1)
                    if j == 5:
                        move(1, n + 1)
                    act.wait_ge(made, c + 1 + START)
                    if j in (0, 2):
                        act.wait_ge(hid_ok, n * 2 + j // 2 + START)
                        act.activation(sg[:, :, :], acc[j % 3][:, :, :], ACT.Silu).then_inc(silu_ok, 1)
                    elif j in (1, 3):
                        h = j // 2
                        act.wait_ge(hid_ok, n * 2 + (h + 1) + START)
                        act.activation(hh[:, 4 * h:4 * h + 4, :], hv[:, :, :], ACT.Copy).then_inc(h_hi, 1)
                        if j == 3:
                            move(0, n + 1)
                    else:
                        half = j - 4
                        act.wait_ge(added[u], i * 32 + ZEROED)
                        out = acc[j % 3][:, :, :].rearrange("p (t x) c -> p t (x c)", t=2)
                        for t in range(2):
                            ins = act.activation(rows[u][t][:, half * W:(half + 1) * W], out[:, t, :], ACT.Copy, scale=gsc[u][:, t:t + 1])
                        ins.then_inc(rows_ok, 1)
            experts_of(act, body)

        @block.vector
        def _(ve):
            def lists(v, n):
                for t in range(2):
                    ve.tensor_copy(offs[v][t][:, :], slots[:, ds(n, 1), t]).then_inc(lists_ok, 1)
                ve.tensor_copy(gsc[v][:, 0:1], gates[:, ds(n, 1), 0]).then_inc(lists_ok, 1)
                ve.tensor_copy(gsc[v][:, 1:2], gates[:, ds(n, 1), 1]).then_inc(lists_ok, 1)

            def split(s, c):
                ve.wait_ge(w_hi, c + 1 + START)
                ve.tensor_tensor(wl[s][:, :, :], raw[s][:, :, :], wh[s][:, :, :], ALU.subtract).then_inc(w_lo, 1)

            def low(t, n):
                ve.wait_ge(x_hi, n * 2 + (t + 1) + START)
                c = slice(t * P, (t + 1) * P)
                ve.tensor_tensor(xl[:, :, c], hx[:, :, c], xh[:, :, c], ALU.subtract).then_inc(x_lo, 1)
            ve.wait_ge(const_in, 16 * 6 + START)
            ve.tensor_scalar(scale1[:, :], mod[:, 1, :], 1.0, None, ALU.add).then_inc(setup, 1)
            ve.wait_ge(setup, 1 + START)
            ve.tensor_tensor(scale[:, :], scale1[:, :], gain[:, :], ALU.mult).then_inc(setup, 1)
            lists(0, 0)
            split(0, 0)
            low(0, 0)
            low(1, 0)

            def body(u, i, n):
                for j in range(NC):
                    c = n * NC + j
                    split(1 - j % 2, c + 1)
                    if j in (1, 3):
                        h = j // 2
                        ve.wait_ge(made, c + 1 + START)
                        ve.wait_ge(silu_ok, n * 2 + (h + 1) + START)
                        ve.wait_ge(h_lo, n * 2 + h + START)
                        ve.tensor_tensor(hv[:, :, :], sg[:, :, :], acc[j % 3][:, :, :], ALU.mult).then_inc(hid_ok, 1)
                        ve.wait_ge(h_hi, n * 2 + (h + 1) + START)
                        ve.tensor_tensor(hl[:, 4 * h:4 * h + 4, :], hv[:, :, :], hh[:, 4 * h:4 * h + 4, :], ALU.subtract).then_inc(h_lo, 1)
                    if j == 2:
                        ve.wait_ge(added[1 - u], i * 32 + 32 * u + ZEROED)
                        ve.sem_inc(spent_v, 1)
                        lists(1 - u, (n + 1) % NE)
                    if j in (4, 5):
                        low(j - 4, n + 1)
            experts_of(ve, body)


def output(nc, T):
    NL, B = LAT // P, 4
    with Room(nc, "out") as room:
        sb, sem = room.sb, room.sem
        m, x, mn, o, sq = [[sb(f"{n}{u}", [P, D]) for u in range(B)] for n in ("m", "x", "mn", "o", "sq")]
        g2, ng, gg, eps = sb("g2", [P, D]), sb("ng", [P, D]), sb("gg", [P, D]), sb("eps", [P, 1])
        ss, rt, rs = [[sb(f"{n}{u}", [P, 1]) for u in range(B)] for n in ("ss", "rt", "rs")]
        rows_in, out = [[sem(f"{n}{u}") for u in range(B)] for n in ("rows_in", "out")]
        const_in, gg_ok, sums, rooted, rec, mn_ok, o_ok, spent = [sem(n) for n in ("const_in", "gg_ok", "sums", "rooted", "rec", "mn_ok", "o_ok", "spent")]
        block = room.block()

        @block.sync
        def _(sp):
            sp.dma_start(g2[:, :], T["mod_rows"][0:1, 5 * D:6 * D].to_broadcast([P, D])).then_inc(const_in, 16)
            sp.dma_start(ng[:, :], T["norm_g"][0, 3:4, :].to_broadcast([P, D])).then_inc(const_in, 16)

            def load(u, at):
                sp.dma_start(m[u][:, :], T["moe"][ds(at, P), :]).then_inc(rows_in[u], 16)
                sp.dma_start(x[u][:, :], T["x1"][ds(at, P), :]).then_inc(rows_in[u], 16)
            for u in range(B):
                load(u, u * P)
            with sp.Fori(0, NL // B - 1) as i:
                for u in range(B):
                    at = sp.snap(i * (B * P) + (B + u) * P)
                    here = sp.snap(i * (B * P) + u * P)
                    sp.wait_ge(o_ok, sp.snap(i * B + (u + 1) + START))
                    sp.sem_inc(spent, 1)
                    sp.dma_start(T["out"][ds(here, P), :], o[u][:, :]).then_inc(out[u], 16)
                    load(u, at)
            for u in range(B):
                sp.wait_ge(o_ok, NL - B + 1 + u + START)
                sp.dma_start(T["out"][LAT + (u - B) * P:LAT + (u - B + 1) * P, :], o[u][:, :]).then_inc(out[u], 16)
            for u in range(B):
                sp.wait_ge(out[u], 16 * (NL // B) + START)

        @block.scalar
        def _(act):
            act.wait_ge(gg_ok, 1 + START)
            with act.Fori(0, NL // B) as i:
                for u in range(B):
                    act.wait_ge(rows_in[u], i * 32 + 32 + START)
                    act.activation(sq[u][:, :], m[u][:, :], ACT.Square, accum_out=ss[u][:, :]).then_inc(sums, 1)
                for u in range(B):
                    act.wait_ge(sums, i * B + (u + 1) + START)
                    act.wait_ge(rec, i * B + START)
                    act.activation(rt[u][:, :], ss[u][:, :], ACT.Sqrt, scale=1.0 / D, bias=eps[:, :]).then_inc(rooted, 1)

        @block.vector
        def _(ve):
            ve.memset(eps[:, :], EPS)
            ve.wait_ge(const_in, 32 + START)
            ve.tensor_tensor(gg[:, :], g2[:, :], ng[:, :], ALU.mult).then_inc(gg_ok, 1)
            ve.wait_ge(gg_ok, 1 + START)
            with ve.Fori(0, NL // B) as i:
                for u in range(B):
                    n = i * B + u
                    ve.wait_ge(rooted, n + 1 + START)
                    ve.reciprocal(rs[u][:, :], rt[u][:, :]).then_inc(rec, 1)
                    ve.wait_ge(rec, n + 1 + START)
                    ve.scalar_tensor_tensor(mn[u][:, :], m[u][:, :], rs[u][:, 0:1], gg[:, :], ALU.mult, ALU.mult).then_inc(mn_ok, 1)
                    ve.wait_ge(mn_ok, n + 1 + START)
                    ve.wait_ge(out[u], i * 16 + START)
                    ve.tensor_tensor(o[u][:, :], mn[u][:, :], x[u][:, :], ALU.add).then_inc(o_ok, 1)


def shape_constants():
    f = np.float32
    out = {"ident": np.eye(P, dtype=f)}
    t = np.arange(LAT)
    inv = 10000.0 ** (-np.arange(32, dtype=f) / 32)
    ang = np.concatenate([(t // 64)[:, None] * inv, (t % 64)[:, None] * inv], -1).astype(f)
    out["cosT"] = np.tile(np.cos(ang).T, (2, 1)).astype(f)
    out["sinT"] = np.tile(np.sin(ang).T, (2, 1)).astype(f)
    s, u = np.arange(P)[:, None], np.arange(P)[None, :]
    quad, level, first = np.zeros((P, 2, 4, P), f), np.zeros((P, 2, 6, P), f), np.zeros((P, 2, P), f)
    for d in range(2):
        later = (u > s) if d == 0 else (u < s)
        for x in range(4):
            quad[:, d, x] = later | (x % 2 == 1) & (u == s)
        for l in range(7):
            b = 1 << l
            near = (s // (2 * b) == u // (2 * b)) & (s // b != u // b) & later
            if l == 0:
                first[:, d] = near
            else:
                level[:, d, l - 1] = near.T
    out.update(quad=quad, level=level, first=first)
    out["head_ones"] = np.kron(np.eye(2), np.ones((64, 64))).astype(f)
    out["head_ones2"] = np.repeat(np.eye(2, dtype=f), 64, 0)
    out["ident2"] = np.tile(np.eye(64, dtype=f), (2, 1))
    scanm = np.ones((P, 4, P), f)
    scanm[:, :, 0] = 0
    out["scanm"] = scanm
    out["tail_pos"] = np.stack([P - 1 - np.arange(P), np.arange(P)], 1).astype(f)
    rel = np.zeros((P, 6, P), f)
    rel[:, 0], rel[:, 1] = np.maximum(u - s, 0), np.maximum(s - u, 0)
    rel[:, 2], rel[:, 3] = u >= s, s >= u
    rel[:, 4], rel[:, 5] = u + 1, P - u
    out["rel"] = rel
    out["same_expert"] = (s // 8 == u // 8).astype(f)
    out["segments_before"] = ((s // 8 == u // 8) & (s < u)).astype(f)
    out["iota"] = np.tile(np.arange(CAP, dtype=f), (P, 1))
    out["bits"] = np.tile(1 << np.arange(29, -1, -1, dtype=np.int32), (P, 1))
    ids = np.zeros((P, 2, P, 2), f)
    ids[..., 0] = (np.arange(P) % 8 * 2)[None, None, :] + np.arange(2)[None, :, None]
    ids[..., 1] = np.arange(P)[:, None, None]
    out["token_ids"] = ids
    return out


INPUTS = ("c", "c_ctx", "b_mod", "norm_g", "ret_log_decay", "ret_gn_g", "rwkv_mu", "rwkv_k_k", "rwkv_k_a", "rwkv_r_k", "rwkv_w0",
          "rwkv_w2", "rwkv_a0", "rwkv_a2", "rwkv_g2", "rwkv_ln_g", "rwkv_ln_b", "w_br_ret", "w_br_rwkv", "w_out", "w_router")

SCRATCH = {"mod_rows": [2, MOD], "zT": [NZ * P, TOK], "kS": [HALF, TOK], "kkn": [HALF, TOK], "kka": [HALF, TOK], "vS": [HALF, TOK],
           "rS": [HALF, TOK], "rrk": [HALF, TOK], "gT": [HALF, LAT], "waS": [P, TOK], "y": [2, TOK, HALF], "bonus": [2, TOK, WH],
           "kTr": [HALF, TOK], "qTr": [HALF, TOK], "Rb": [NT, P, RH, P], "yrT": [HALF, LAT], "ywT": [HALF, LAT], "mixT": [D, LAT],
           "x1": [LAT, D], "xh": [LAT, D], "affT": [NE, LAT], "gates": [P, NE, 2], "moe": [LAT, D]}


def columns():
    q0 = 4 * HALF + P
    pairs = np.arange(HALF).reshape(2, 2, 2, 64).transpose(0, 2, 1, 3).reshape(-1)
    return np.concatenate([pairs, np.arange(HALF, q0), q0 + 3 * HALF + np.arange(P), q0 + pairs, q0 + 2 * HALF + np.arange(HALF),
                           q0 + HALF + np.arange(HALF), q0 + 3 * HALF + P + np.arange(2 * D)])


def layout(a):
    out = {n: a[n] for n in INPUTS}
    out["w_mod"] = a["w_mod"][0].reshape(KT, P, MOD // 512, 512).transpose(2, 1, 0, 3)
    out["tokens"] = np.concatenate([a["ctx"][0], a["x"][0]])
    w = a["w_in"][0][:, columns()].reshape(KT, P, NZ, P).transpose(2, 1, 0, 3)
    out["w_z"] = np.concatenate([w, np.zeros((2, P, KT, P), w.dtype)])
    g, u, d = [a[n][0].reshape(NE, 8, P, 2, 512).transpose(0, 3, 2, 1, 4) for n in ("w_gate", "w_up", "w_down")]
    out["w_x"] = np.stack([g[:, 0], u[:, 0], g[:, 1], u[:, 1], d[:, 0], d[:, 1]], 1).reshape(NE * 6, P, 8, 512)
    out.update(shape_constants())
    return {n: np.ascontiguousarray(v) for n, v in out.items()}


STAGES = (modulation, projection, rwkv_channels, rwkv_chunks, rotate, retention_backward, retention_forward, rwkv_output,
          branch_products, mixer_output, router, choose, experts, output)


def build(nc, arrays):
    T = {n: nc.dram_tensor(f"in_{n}", list(v.shape), I32 if v.dtype == np.int32 else F32, kind="ExternalInput").ap()
         for n, v in arrays.items()}
    for n, shape in SCRATCH.items():
        T[n] = nc.dram_tensor(f"s_{n}", shape, F32).ap()
    T["slots"] = nc.dram_tensor("s_slots", [P, NE, 2], I32).ap()
    T["out"] = nc.dram_tensor("out", [LAT, D], F32, kind="ExternalOutput").ap()
    for stage in STAGES:
        stage(nc, T)


def kernel(**inputs):
    import concourse.bacc as bacc
    from concourse.bass_utils import run_bass_kernel_spmd

    arrays = layout({n: np.asarray(v) for n, v in inputs.items()})
    nc = bacc.Bacc("TRN2", target_bir_lowering=False, num_devices=1)
    build(nc, arrays)
    nc.finalize()
    res = run_bass_kernel_spmd(nc, [{f"in_{n}": v for n, v in arrays.items()}], core_ids=[0])
    return res.results[0]["out"].reshape(1, LAT, D)
```
